# Optimizing a Trainium2 kernel written in Bass

```python
import jax, jax.numpy as jnp
from jax import lax
import numpy as np

D_MODEL = 2048
BATCH = 1
SEQ = 256
DEPTH = 1
DEC_BATCH = 8
DEC_SEQ = 8
PAST_LEN = 1024
PAGE_SIZE = 128

HEAD_DIM = 64
A_Q_HEADS = 16
A_KV_HEADS = 2
A_GROUP = A_Q_HEADS // A_KV_HEADS
A_WINDOW = 128
B_PATTERNS = ((128, 1), (512, 4), (2048, 16))
N_B_GROUPS = len(B_PATTERNS)
B_HEADS = 8
B_KEYS = 128
BLOCK = 128
D_FF = 4 * D_MODEL
ROPE_THETA = 10000.0
ALPHA = (2.0 * DEPTH) ** 0.25
BETA = (8.0 * DEPTH) ** -0.25
LN_EPS = 1e-5
NEG = -1e30

A_Q_W = A_Q_HEADS * HEAD_DIM
A_KV_W = A_KV_HEADS * HEAD_DIM
B_W = N_B_GROUPS * B_HEADS * HEAD_DIM
B_OUT_W = B_HEADS * HEAD_DIM
PROJ_W = A_Q_W + 2 * A_KV_W + 3 * B_W + 2 * D_MODEL

kernel_name = 'hybrid_swa_sink_dilated_decoder_step'

def _col_splits():
    sizes = (A_Q_W, A_KV_W, A_KV_W, B_W, B_W, B_W, D_MODEL)
    return [int(s) for s in np.cumsum(sizes)]

def layer_norm(x, g, b):
    xf = x.astype(jnp.float32)
    mu = xf.mean(-1, keepdims=True)
    var = jnp.square(xf - mu).mean(-1, keepdims=True)
    return ((xf - mu) * lax.rsqrt(var + LN_EPS) * g + b).astype(x.dtype)

def rope(x, pos):
    half = HEAD_DIM // 2
    inv = 1.0 / (ROPE_THETA ** (jnp.arange(half, dtype=jnp.float32) / half))
    ang = pos.astype(jnp.float32)[:, None] * inv[None, :]
    cos, sin = jnp.cos(ang)[:, None, :], jnp.sin(ang)[:, None, :]
    xf = x.astype(jnp.float32)
    x1, x2 = xf[..., :half], xf[..., half:]
    return jnp.concatenate([x1 * cos - x2 * sin, x2 * cos + x1 * sin], -1).astype(x.dtype)

def _softmax_stats(scores, sink):
    lse = jax.nn.logsumexp(scores, axis=-1, keepdims=True)
    if sink is not None:
        lse = jnp.logaddexp(lse, sink)
    return jnp.exp(scores - lse), lse[..., 0]

def banded_window_attn(q, k, v, dilation, sink=None):
    N, S, KV, G, HD = q.shape
    L = S // dilation
    M = N * dilation

    def to_residue(t):
        t = t.reshape((N, L, dilation) + t.shape[2:])
        t = jnp.moveaxis(t, 2, 1)
        return t.reshape((M, L) + t.shape[3:])

    nb = -(-L // BLOCK)
    pad = nb * BLOCK - L

    def blocks(t):
        t = jnp.pad(t, [(0, 0), (0, pad)] + [(0, 0)] * (t.ndim - 2))
        return t.reshape((M, nb, BLOCK) + t.shape[2:])

    qb = blocks(to_residue(q))
    kb = blocks(to_residue(k))
    vb = blocks(to_residue(v))
    kk = jnp.concatenate([jnp.concatenate([jnp.zeros_like(kb[:, :1]), kb[:, :-1]], 1), kb], 2)
    vv = jnp.concatenate([jnp.concatenate([jnp.zeros_like(vb[:, :1]), vb[:, :-1]], 1), vb], 2)
    scores = jnp.einsum('mbqkgd,mbskd->mbkgqs', qb.astype(jnp.float32), kk.astype(jnp.float32)) * (HEAD_DIM ** -0.5)
    qi = np.arange(BLOCK)[:, None]
    sj = np.arange(2 * BLOCK)[None, :]
    dist = BLOCK + qi - sj
    band = (dist >= 0) & (dist < B_KEYS)
    first = (np.arange(nb)[:, None, None] > 0) | (sj[None] >= BLOCK)
    mask = band[None] & first
    scores = jnp.where(mask[None, :, None, None], scores, NEG)
    sink_b = None if sink is None else sink.astype(jnp.float32)[None, None, :, :, None, None]
    p, lse = _softmax_stats(scores, sink_b)
    out = jnp.einsum('mbkgqs,mbskd->mbqkgd', p.astype(vv.dtype), vv)
    lse = jnp.moveaxis(lse, -1, 2)

    def from_residue(t):
        t = t.reshape((M, nb * BLOCK) + t.shape[3:])[:, :L]
        t = t.reshape((N, dilation, L) + t.shape[2:])
        t = jnp.moveaxis(t, 1, 2)
        return t.reshape((N, S) + t.shape[3:])

    return from_residue(out), from_residue(lse)

def gathered_window_attn(q, kv_buf, dilation, sink=None):
    N, T, KV, G, HD = q.shape
    Lb = kv_buf.shape[1] - T
    idx = Lb + np.arange(T)[:, None] - dilation * np.arange(B_KEYS)[None, :]
    valid = idx >= 0
    g = jnp.take(kv_buf, np.clip(idx, 0, None).reshape(-1), axis=1)
    g = g.reshape((N, T, B_KEYS) + kv_buf.shape[2:])
    kg, vg = g[:, :, :, 0], g[:, :, :, 1]
    scores = jnp.einsum('ntkgd,ntjkd->ntkgj', q.astype(jnp.float32), kg.astype(jnp.float32)) * (HEAD_DIM ** -0.5)
    scores = jnp.where(valid[None, :, None, None, :], scores, NEG)
    sink_b = None if sink is None else sink.astype(jnp.float32)[None, None, :, :, None]
    p, lse = _softmax_stats(scores, sink_b)
    out = jnp.einsum('ntkgj,ntjkd->ntkgd', p.astype(vg.dtype), vg)
    return out, lse

def project_inputs(x, pos, w_in):
    N, S, _ = x.shape
    h = jnp.einsum('bsd,de->bse', x, w_in)
    qa, ka, va, qb, kb, vb, ga, gb = jnp.split(h, _col_splits(), axis=-1)
    qa = rope(qa.reshape(N, S, A_Q_HEADS, HEAD_DIM), pos).reshape(N, S, A_KV_HEADS, A_GROUP, HEAD_DIM)
    ka = rope(ka.reshape(N, S, A_KV_HEADS, HEAD_DIM), pos)
    va = va.reshape(N, S, A_KV_HEADS, HEAD_DIM)
    nbh = N_B_GROUPS * B_HEADS
    qb = rope(qb.reshape(N, S, nbh, HEAD_DIM), pos).reshape(N, S, N_B_GROUPS, B_HEADS, HEAD_DIM)
    kb = rope(kb.reshape(N, S, nbh, HEAD_DIM), pos).reshape(N, S, N_B_GROUPS, B_HEADS, HEAD_DIM)
    vb = vb.reshape(N, S, N_B_GROUPS, B_HEADS, HEAD_DIM)
    return qa, ka, va, qb, kb, vb, jax.nn.sigmoid(ga), jax.nn.sigmoid(gb)

def combine_dilations(outs, lses):
    w = jax.nn.softmax(jnp.stack(lses, 0), axis=0)
    o = jnp.sum(w[..., None] * jnp.stack(outs, 0).astype(jnp.float32), axis=0).astype(outs[0].dtype)
    N, S = o.shape[:2]
    return o.reshape(N, S, B_OUT_W)

def finish_layer(x, o_a, o_b, ga, gb, w_branch_a, w_branch_b, w_out, ln1_g, ln1_b,
                 w_ff1, b_ff1, w_ff2, b_ff2, ln2_g, ln2_b):
    N, S, _ = x.shape
    br_a = jnp.einsum('bse,ed->bsd', o_a.reshape(N, S, A_Q_W), w_branch_a)
    br_b = jnp.einsum('bse,ed->bsd', o_b, w_branch_b)
    mix = jnp.einsum('bsd,de->bse', ga * br_a + gb * br_b, w_out)
    h = layer_norm(ALPHA * x + mix, ln1_g, ln1_b)
    u = jnp.square(jax.nn.relu(jnp.einsum('bsd,df->bsf', h, w_ff1) + b_ff1))
    f = jnp.einsum('bsf,fd->bsd', u, w_ff2) + b_ff2
    return layer_norm(ALPHA * h + f, ln2_g, ln2_b)

def setup_inputs(seed: int = 0) -> dict:
    key = jax.random.key(seed)
    ks = jax.random.split(key, 19)
    f32 = jnp.float32

    def nrm(k, shape, s):
        return jax.random.normal(k, shape, f32) * s

    la = min(A_WINDOW, PAST_LEN)
    lb = [min(w, PAST_LEN) for (w, _) in B_PATTERNS]
    v_scale = np.ones((PROJ_W,), np.float32)
    va0 = A_Q_W + A_KV_W
    v_scale[va0:va0 + A_KV_W] = BETA
    vb0 = A_Q_W + 2 * A_KV_W + 2 * B_W
    v_scale[vb0:vb0 + B_W] = BETA
    return {
        'x_prompt': nrm(ks[0], (BATCH, SEQ, D_MODEL), 1.0),
        'x_sample': nrm(ks[1], (DEC_BATCH, DEC_SEQ, D_MODEL), 1.0),
        'cache_a_kv': nrm(ks[2], (DEPTH, DEC_BATCH, la, 2, A_KV_HEADS, HEAD_DIM), 1.0),
        'cache_b1_kv': nrm(ks[3], (DEPTH, DEC_BATCH, lb[0], 2, B_HEADS, HEAD_DIM), 1.0),
        'cache_b2_kv': nrm(ks[4], (DEPTH, DEC_BATCH, lb[1], 2, B_HEADS, HEAD_DIM), 1.0),
        'cache_b3_kv': nrm(ks[5], (DEPTH, DEC_BATCH, lb[2], 2, B_HEADS, HEAD_DIM), 1.0),
        'w_in': nrm(ks[6], (DEPTH, D_MODEL, PROJ_W), D_MODEL ** -0.5) * jnp.asarray(v_scale),
        'a_sinks': nrm(ks[7], (DEPTH, A_KV_HEADS, A_GROUP), 0.5),
        'w_branch_a': nrm(ks[8], (DEPTH, A_Q_W, D_MODEL), BETA * A_Q_W ** -0.5),
        'w_branch_b': nrm(ks[9], (DEPTH, B_OUT_W, D_MODEL), BETA * B_OUT_W ** -0.5),
        'w_out': nrm(ks[10], (DEPTH, D_MODEL, D_MODEL), BETA * D_MODEL ** -0.5),
        'ln1_g': 1.0 + nrm(ks[11], (DEPTH, D_MODEL), 0.02),
        'ln1_b': nrm(ks[12], (DEPTH, D_MODEL), 0.02),
        'w_ff1': nrm(ks[13], (DEPTH, D_MODEL, D_FF), BETA * D_MODEL ** -0.5),
        'b_ff1': nrm(ks[14], (DEPTH, D_FF), 0.02),
        'w_ff2': nrm(ks[15], (DEPTH, D_FF, D_MODEL), BETA * D_FF ** -0.5),
        'b_ff2': nrm(ks[16], (DEPTH, D_MODEL), 0.02),
        'ln2_g': 1.0 + nrm(ks[17], (DEPTH, D_MODEL), 0.02),
        'ln2_b': nrm(ks[18], (DEPTH, D_MODEL), 0.02),
    }

def reference(x_prompt, x_sample, cache_a_kv, cache_b1_kv, cache_b2_kv, cache_b3_kv,
              w_in, a_sinks, w_branch_a, w_branch_b, w_out, ln1_g, ln1_b,
              w_ff1, b_ff1, w_ff2, b_ff2, ln2_g, ln2_b):
    S = x_prompt.shape[1]
    T = x_sample.shape[1]
    pos_p = jnp.arange(S)
    pos_s = PAST_LEN + jnp.arange(T)
    b_caches = (cache_b1_kv, cache_b2_kv, cache_b3_kv)
    hp, hs = x_prompt, x_sample
    a_p, a_s = [], []
    b_p = [[] for _ in B_PATTERNS]
    b_s = [[] for _ in B_PATTERNS]
    for l in range(DEPTH):
        rest = (w_branch_a[l], w_branch_b[l], w_out[l], ln1_g[l], ln1_b[l],
                w_ff1[l], b_ff1[l], w_ff2[l], b_ff2[l], ln2_g[l], ln2_b[l])
        qa, ka, va, qb, kb, vb, ga, gb = project_inputs(hp, pos_p, w_in[l])
        o_a, _ = banded_window_attn(qa, ka, va, 1, a_sinks[l])
        outs, lses = [], []
        for g, (win, dil) in enumerate(B_PATTERNS):
            o, lse = banded_window_attn(qb[:, :, g, :, None, :], kb[:, :, g], vb[:, :, g], dil)
            outs.append(o)
            lses.append(lse)
            b_p[g].append(jnp.stack([kb[:, :, g], vb[:, :, g]], 2)[:, S - min(win, S):])
        a_p.append(jnp.stack([ka, va], 2)[:, S - min(A_WINDOW, S):])
        o_b = combine_dilations(outs, lses)
        hp_next = finish_layer(hp, o_a, o_b, ga, gb, *rest)
        qa, ka, va, qb, kb, vb, ga, gb = project_inputs(hs, pos_s, w_in[l])
        buf_a = jnp.concatenate([cache_a_kv[l], jnp.stack([ka, va], 2)], 1)
        o_a, _ = gathered_window_attn(qa, buf_a, 1, a_sinks[l])
        a_s.append(buf_a[:, buf_a.shape[1] - min(A_WINDOW, PAST_LEN + T):])
        outs, lses = [], []
        for g, (win, dil) in enumerate(B_PATTERNS):
            buf = jnp.concatenate([b_caches[g][l], jnp.stack([kb[:, :, g], vb[:, :, g]], 2)], 1)
            o, lse = gathered_window_attn(qb[:, :, g, :, None, :], buf, dil)
            outs.append(o)
            lses.append(lse)
            b_s[g].append(buf[:, buf.shape[1] - min(win, PAST_LEN + T):])
        o_b = combine_dilations(outs, lses)
        hs = finish_layer(hs, o_a, o_b, ga, gb, *rest)
        hp = hp_next
    return (hp, hs,
            jnp.stack(a_p, 0), jnp.stack(a_s, 0),
            jnp.stack(b_p[0], 0), jnp.stack(b_s[0], 0),
            jnp.stack(b_p[1], 0), jnp.stack(b_s[1], 0),
            jnp.stack(b_p[2], 0), jnp.stack(b_s[2], 0))


_drawn_inputs = setup_inputs


def setup_inputs(seed=0):
    import zlib

    import numpy as np

    out = dict(_drawn_inputs(seed))
    spreads = {}
    factors = {'a_sinks': 200.0,
     'w_branch_b': 3.068,
     'ln1_g': 7.985,
     'ln1_b': 8.049,
     'b_ff1': 6.785,
     'b_ff2': 54.753,
     'ln2_g': 22.72,
     'ln2_b': 22.764,
     'w_branch_a': 2.791}
    for name, (base, spread) in spreads.items():
        noise = np.random.default_rng([zlib.crc32(name.encode()), seed]).standard_normal(out[name].shape)
        drawn = base * np.exp(spread * noise) if base else spread * noise
        out[name] = __import__('jax').numpy.asarray(drawn.astype(out[name].dtype))
    for name, factor in factors.items():
        out[name] = (out[name] * factor).astype(out[name].dtype)
    return out
```

```python
from contextlib import ExitStack

import concourse.bass as bass
import numpy as np
from concourse import mybir

F32 = mybir.dt.float32
F32R = mybir.dt.float32r
ACT = mybir.ActivationFunctionType
ALU = mybir.AluOpType
AX = mybir.AxisListType

P = 128
D = 2048
DFF = 4 * D
SEQ, DB, DT, PAST = 256, 8, 8, 1024
NTOK = SEQ + DB * DT
HD = 64
QH_A, KV_A, H_B, NG = 16, 2, 8, 3
GW = 256
KT = 4
RING = 4
NEG = -1e30
SCALE = HD ** -0.5
ALPHA = 2.0 ** 0.25
EPS = 1e-5
THETA = 10000.0
WIN = (128, 512, 2048)
DIL = (1, 4, 16)
KVW = 1664
CK = 9


def program(nc, a, o):
    ctx = ExitStack()
    with ctx:
        def sb(name, shape, dt=F32):
            return ctx.enter_context(nc.sbuf_tensor("s_" + name, shape, dt))

        def sem(name):
            return ctx.enter_context(nc.semaphore(name))

        raw = sb("raw", [P, RING, KT, GW])
        whi = sb("whi", [P, RING, KT, GW], F32R)
        wlo = sb("wlo", [P, RING, KT, GW], F32R)

        def overlay(*sets):
            made, base = [], []
            for k, tensors in enumerate(sets):
                with ExitStack() as own:
                    made.append([own.enter_context(nc.sbuf_tensor("s_" + n, s, d)) for n, s, d in tensors])
            size = [sum(int(np.prod(s[1:])) for _, s, _ in t) for t in sets]
            ctx.enter_context(nc.sbuf_tensor(f"hold_{len(made)}_{sets[0][0][0]}", [P, max(size)], F32))
            return made

        (xhi, xlo), (kcache, vcache), (ohi, olo), (hhi, hlo) = overlay(
            [("xhi", [P, 16, NTOK], F32R), ("xlo", [P, 16, NTOK], F32R)],
            [("kcache", [P, 4, CK, P], F32), ("vcache", [P, CK, 512], F32)],
            [("ohi", [P, 12, NTOK], F32R), ("olo", [P, 12, NTOK], F32R)],
            [("hhi", [P, 16, NTOK], F32R), ("hlo", [P, 16, NTOK], F32R)],
        )
        (xraw,), (vnat, qT, kTb, kTa), (r, mhi, mlo), (_, uhi, ulo) = overlay(
            [("xraw", [P, 16, NTOK], F32)],
            [("vnat", [P, 3, KVW], F32), ("qT", [P, 20, NTOK], F32),
             ("kTb", [P, 12, NTOK], F32), ("kTa", [P, 3, NTOK], F32)],
            [("r", [P, 16, NTOK], F32), ("mhi", [P, 16, NTOK], F32R), ("mlo", [P, 16, NTOK], F32R)],
            [("r_again", [P, 16, NTOK], F32), ("uhi", [P, 16, NTOK], F32R), ("ulo", [P, 16, NTOK], F32R)],
        )
        (tT, rot, kst, gstage), (QB, KB, VB, QA, QbS, QaS, kca, vca, S, PT), (gt, xres, t1, t2, lnrow) = overlay(
            [("tT", [P, 2, 2, NTOK], F32), ("rot", [P, 2, NTOK], F32), ("kst", [P, 2, 3, GW], F32),
             ("gstage", [P, 2, 2, NTOK], F32)],
            [("QB", [P, 3, 256], F32), ("KB", [P, 3, 256], F32), ("VB", [P, 2, 3, P], F32),
             ("QA", [P, 2, 256], F32), ("QbS", [P, 3, 4, P], F32), ("QaS", [P, P], F32),
             ("kca", [P, P], F32), ("vca", [P, P], F32), ("S", [P, 2, 768], F32), ("PT", [P, 768], F32)],
            [("gt", [P, 4, 2, NTOK], F32), ("xres", [P, 2, 2, NTOK], F32), ("t1", [P, 2, NTOK], F32),
             ("t2", [P, 2, 2, NTOK], F32), ("lnrow", [P, 3, NTOK], F32)],
        )
        qTa, qTb = qT[:, 0:8], qT[:, 8:20]
        oT = sb("oT", [P, 12, NTOK])
        rope = sb("rope", [P, 2, NTOK])
        ident = sb("ident", [P, P])
        onesD = sb("onesD", [P, P])
        mask_p = sb("mask_p", [P, 3, 384])
        mask_c = sb("mask_c", [P, 4, P])
        mask_n = sb("mask_n", [P, 4, 120])
        sink_p = sb("sink_p", [P, QH_A])
        sink_s = sb("sink_s", [P, 2])
        vecs = sb("vecs", [P, 5 * 16 + 64])
        st = sb("st", [P, 2, 16])
        ln1g, ln1b, ln2g, ln2b, bff2 = (vecs[:, 16 * k:16 * k + 16] for k in range(5))
        bff1 = vecs[:, 80:144]

        psM = [ctx.enter_context(nc.psum_tensor(f"psM{k}", [P, 2, 512], F32)) for k in range(2)]
        psT = ctx.enter_context(nc.psum_tensor("psT", [P, 2, 512], F32))
        psO = ctx.enter_context(nc.psum_tensor("psO", [P, 2, 512], F32))
        psTf = psT[:, :, :].rearrange("p a b -> p (a b)")

        gates_d = nc.dram_tensor("gates_scratch", [32, P, NTOK], F32, kind="Internal").ap()
        kvn_d = nc.dram_tensor("kv_scratch", [NTOK, 2 * KVW], F32, kind="Internal").ap()


        loaded = [sem(f"loaded{k}") for k in range(RING)]
        hi_done, lo_done = sem("hi_done"), sem("lo_done")
        chunk_done = sem("chunk_done")
        evac = [sem("evac0"), sem("evac1")]
        const_in = sem("const_in")
        x_in = [sem(f"x_in{k}") for k in range(4)]
        x_hi, x_lo = sem("x_hi"), sem("x_lo")
        rot_ready, rope_a, rope_b = sem("rot_ready"), sem("rope_a"), sem("rope_b")
        kcopy, dup_ready = sem("kcopy"), sem("dup_ready")
        turned, turned_out = sem("turned"), sem("turned_out")
        kv_stored = [sem("kv_stored0"), sem("kv_stored1")]
        gate_stored = [sem("gate_stored0"), sem("gate_stored1")]
        out_kv, out_cache, y_out = sem("out_kv"), sem("out_cache"), sem("y_out")
        zeroed, staged = sem("zeroed"), sem("staged")
        kc_in, vc_in = sem("kc_in"), sem("vc_in")
        scores, masked, maxed, sinkmax, shifted = (sem(n) for n in ("scores", "masked", "maxed", "sinkmax", "shifted"))
        exped, denom, recip, normed = (sem(n) for n in ("exped", "denom", "recip", "normed"))
        pT, pT_out, pv, o_out = (sem(n) for n in ("pT", "pT_out", "pv", "o_out"))
        o_hi, o_lo = sem("o_hi"), sem("o_lo")
        g_in = [sem(f"g_in{k}") for k in range(4)]
        m_sum, m_hi, m_lo = sem("m_sum"), sem("m_hi"), sem("m_lo")
        xr_in = [sem("xr_in0"), sem("xr_in1")]
        ln_dve, ln_pe, ln_act = sem("ln_dve"), sem("ln_pe"), sem("ln_act")
        h_hi, h_lo, r_init = sem("h_hi"), sem("h_lo"), sem("r_init")
        u_done, u_hi, u_lo = sem("u_done"), sem("u_hi"), sem("u_lo")

        G_QB, G_KVA, G_K, G_V, G_G, G_BR, G_WO, G_FF = 4, 10, 11, 17, 23, 39, 55, 63
        C_BR = 4 * G_BR
        C_WO = C_BR + 24
        C_FF = C_WO + 32
        G_BLK, C_BLK = 16, 64
        C_KVA, C_QB, C_K = QH_A * HD, QH_A * HD + 256, QH_A * HD + 256 + NG * 512
        C_GATE = C_K + 2 * NG * 512

        w_in, w_a, w_b, w_out = (a[n][0] for n in ("w_in", "w_branch_a", "w_branch_b", "w_out"))
        w1, w2 = a["w_ff1"][0], a["w_ff2"][0]

        def projections(eng, step):
            step(0, 0, 0, "q", None)
            step(1, 0, 1, "q", None)
            with eng.Fori(0, 4) as i:
                for c in range(2, 4):
                    step(i * 2 + c, i, c, "q", None)
            step(10, 0, 10, "kva", None)
            step(11, 0, 11, "k", "kva")
            with eng.Fori(0, 2) as i:
                for c in range(12, 14):
                    step(i * 2 + c, i, c, "k", "k")
            step(16, 0, 16, "k", "k")
            step(17, 0, 17, "v", "k")
            with eng.Fori(0, 2) as i:
                for c in range(18, 20):
                    step(i * 2 + c, i, c, "v", "v")
            step(22, 0, 22, "v", "v")
            step(23, 0, 23, "gate", "v")
            step(24, 0, 24, "gate", None)
            with eng.Fori(0, 7) as i:
                for c in range(25, 27):
                    step(i * 2 + c, i, c, "gate", None)

        UNITS = [("B", 0, 0), ("B", 0, 1), ("SB", 0, 0), ("SA", 0, 0), ("A", 0, 0), ("A", 0, 1),
                 ("B", 1, 0), ("B", 1, 1), ("SB", 1, 0), ("SA", 1, 0), ("A", 1, 0), ("A", 1, 1)]
        NU = len(UNITS)
        STAGED = {0: 1, 2: 2, 3: 3, 8: 4, 9: 5}

        block = ctx.enter_context(nc.Block())

        @block.sync
        def _(sp):
            def load(c, slot, w, row, col):
                if not (isinstance(c, int) and c < RING):
                    sp.wait_ge(lo_done, c - (RING - 1))
                src = w[bass.ds(row, KT * P), bass.ds(col, GW)].rearrange("(t p) n -> p t n", p=P)
                sp.dma_start(raw[:, slot], src).then_inc(loaded[slot], 16)

            def load_group(c, w, row, col):
                for j in range(4):
                    load(c + j, j, w, row + j * KT * P, col)

            xv = a["xT"].rearrange("(t p) n -> p t n", p=P)
            for j in range(4):
                sp.dma_start(xraw[:, 4 * j:4 * j + 4], xv[:, 4 * j:4 * j + 4]).then_inc(x_in[j], 16)
                load(j, j, w_in, j * KT * P, 0)
            for dst, name in ((rope, "rope"), (ident, "ident"), (mask_p, "mask_p"), (mask_c, "mask_c"),
                              (mask_n, "mask_n"), (sink_p, "sink_p"), (sink_s, "sink_s"), (vecs, "vecs")):
                sp.dma_start(dst[:], a[name]).then_inc(const_in, 16)
            with sp.Fori(0, 3) as i:
                load_group(i * 4 + 4, w_in, 0, i * GW + GW)
            with sp.Fori(0, 6) as i:
                load_group(i * 4 + 4 * G_QB, w_in, 0, i * GW + C_QB)
            load_group(4 * G_KVA, w_in, 0, C_KVA)
            with sp.Fori(0, 12) as i:
                load_group(i * 4 + 4 * G_K, w_in, 0, i * GW + C_K)
            with sp.Fori(0, 16) as i:
                load_group(i * 4 + 4 * G_G, w_in, 0, i * GW + C_GATE)
            with sp.Fori(0, 2) as i:
                for q in range(4):
                    for j in range(3):
                        load(i * 12 + (C_BR + 3 * q + j), (3 * q + j) % RING, w_b if j == 2 else w_a,
                             0 if j == 2 else j * KT * P, i * (4 * GW) + q * GW)
            with sp.Fori(0, 8) as i:
                load_group(i * 4 + C_WO, w_out, 0, i * GW)
            with sp.Fori(0, 4) as b:
                with sp.Fori(0, 8) as q:
                    load_group(b * C_BLK + q * 4 + C_FF, w1, 0, b * (8 * GW) + q * GW)
                with sp.Fori(0, 8) as q:
                    load_group(b * C_BLK + q * 4 + (C_FF + 32), w2, b * D, q * GW)

        @block.gpsimd
        def _(pool):
            nc.gpsimd.memset(onesD[:], 1.0 / D).then_inc(zeroed, 1)

            def kcopy_step(g, i, c, kind, turn):
                if kind == "k":
                    pool.wait_ge(evac[c % 2], i + (c // 2 + 1))
                    pool.tensor_copy(kTb[:, bass.ds((g - G_K) * 2, 2)], tT[:, c % 2]).then_inc(kcopy, 1)

            kcopy_step(11, 0, 11, "k", None)
            with pool.Fori(0, 2) as i:
                for c in range(12, 14):
                    kcopy_step(i * 2 + c, i, c, "k", None)
            kcopy_step(16, 0, 16, "k", None)

            pool.wait_ge(kv_stored[0], 16 * 14)
            pool.wait_ge(kv_stored[1], 16 * 14)
            kv_rows = kvn_d.rearrange("t (s c) -> t s c", s=2)
            for name, col, wid, win in (("a", 0, 128, 128), ("b1", 128, 512, 128), ("b2", 640, 512, 512), ("b3", 1152, 512, 2048)):
                rows = min(win, SEQ)
                dst = o[name + "_p"][0, 0].rearrange("t s h d -> t s (h d)")
                pool.dma_start(dst, kv_rows[SEQ - rows:SEQ, :, col:col + wid]).then_inc(out_kv, 16)
                keep = min(win, PAST + DT)
                for s in range(2):
                    dst = o[name + "_s"][0, :, keep - DT:keep, s].rearrange("n t h d -> n t (h d)")
                    src = kv_rows[SEQ:NTOK, s, col:col + wid].rearrange("(n t) c -> n t c", n=DB)
                    pool.dma_start(dst, src).then_inc(out_kv, 16)

            def load_k(n):
                pool.dma_start(kcache[:].rearrange("p a c k -> p (a c k)"),
                               a["kT_b"][bass.ds(n, 1)].rearrange("n p k -> (n p) k")).then_inc(kc_in, 16)
                pool.dma_start(kca[:], a["kT_a"][bass.ds(n, 1)].rearrange("n p k -> (n p) k")).then_inc(kc_in, 16)

            def load_v(n):
                for dst, src in ((vca[:], a["v_a"]), (vcache[:].rearrange("p c k -> p (c k)"), a["v_b"])):
                    pool.dma_start(dst, src[bass.ds(n, 1)].rearrange("n p k -> (n p) k")).then_inc(vc_in, 16)

            pool.wait_ge(chunk_done, C_BR)
            pool.wait_ge(turned_out, 13)
            pool.wait_ge(gate_stored[0], 16 * 8)
            pool.wait_ge(gate_stored[1], 16 * 8)
            load_k(0)
            load_v(0)
            with pool.Fori(0, 3) as i:
                for e in range(2):
                    pool.wait_ge(pv, i * NU + (4 + 6 * e))
                    pool.wait_ge(chunk_done, C_BR)
                    load_k(i * 2 + (1 + e))
                    load_v(i * 2 + (1 + e))
            pool.wait_ge(pv, 3 * NU + 4)
            load_k(7)
            load_v(7)

            def load_gates(q, e):
                for k in range(2):
                    pool.dma_start(gt[:, 2 * e + k], gates_d[bass.ds(q * 2 + 16 * k, 2)].rearrange("t p n -> p t n")
                                   ).then_inc(g_in[2 * e + k], 16)

            pool.wait_ge(o_out, 4 * NU)
            pool.wait_ge(pv, 4 * NU)
            load_gates(0, 0)
            load_gates(1, 1)
            with pool.Fori(0, 3) as i:
                for e in range(2):
                    pool.wait_ge(m_sum, i * 2 + (1 + e))
                    pool.wait_ge(pv, 4 * NU)
                    load_gates(i * 2 + (2 + e), e)

            def load_x(q, e):
                pool.dma_start(xres[:, e], a["xT"][bass.ds(q * 256, 256)].rearrange("(t p) n -> p t n", p=P)
                               ).then_inc(xr_in[e], 16)

            load_x(0, 0)
            load_x(1, 1)
            with pool.Fori(0, 3) as i:
                pool.wait_ge(evac[1], i + ((G_WO + 1) // 2))
                pool.wait_ge(pv, 4 * NU)
                load_x(i * 2 + 2, 0)
                pool.wait_ge(evac[0], i + ((G_WO + 1) // 2 + 1))
                pool.wait_ge(pv, 4 * NU)
                load_x(i * 2 + 3, 1)

            with pool.Fori(0, DB) as n:
                pool.wait_ge(lo_done, n * 24 + C_FF)
                pool.wait_ge(pv, 4 * NU)
                for name, win in (("a", 128), ("b1", 128), ("b2", 512), ("b3", 2048)):
                    keep = min(win, PAST + DT)
                    past = min(win, PAST)
                    cache = a[f"cache_{name}_kv"][0]
                    dst = o[name + "_s"][0, bass.ds(n, 1), 0:keep - DT].rearrange("n t s h d -> (n t) (s h d)")
                    src = cache[bass.ds(n, 1), past - (keep - DT):past].rearrange("n t s h d -> (n t) (s h d)")
                    pool.dma_start(dst, src).then_inc(out_cache, 16)
            pool.wait_ge(out_kv, 16 * 12)
            pool.wait_ge(out_cache, 16 * 4 * DB)
            pool.wait_ge(y_out, 16 * 4)

        @block.scalar
        def _(act):
            def split(q, slot, first=False):
                act.wait_ge(loaded[slot], q * 16 + 16)
                if not first:
                    act.wait_ge(chunk_done, q * 4 + (slot - RING + 1))
                act.activation(whi[:, slot], raw[:, slot], ACT.Copy).then_inc(hi_done, 1)

            for j in range(4):
                act.wait_ge(x_in[j], 16)
                act.activation(xhi[:, 4 * j:4 * j + 4], xraw[:, 4 * j:4 * j + 4], ACT.Copy).then_inc(x_hi, 1)
                split(0, j, first=True)

            def turn_out(g, i, c, kind):
                par = c % 2
                act.wait_ge(turned, g - 9)
                ps = psTf[:, 0:768].rearrange("p (c n) -> p c n", c=3)

                def move(dst, dcol, scol, n):
                    act.activation(dst[:, 0:2, dcol], ps[:, 0:2, scol:scol + n], ACT.Copy)
                    return act.activation(dst[0:64, 2, dcol], ps[0:64, 2, scol:scol + n], ACT.Copy)

                def store(src, scol, dcol, n, done=kv_stored[par]):
                    act.dma_start(kvn_d[0:256, bass.ds(dcol, n)].rearrange("(c p) n -> p c n", p=P),
                                  src[:, 0:2, scol]).then_inc(done, 16)
                    act.dma_start(kvn_d[256:NTOK, bass.ds(dcol, n)], src[0:64, 2, scol]).then_inc(done, 16)

                if kind == "kva":
                    move(kst[:, par], slice(0, P), 0, P)
                    move(vnat, slice(0, P), P, P).then_inc(turned_out, 1)
                    act.wait_ge(turned_out, 1)
                    store(kst[:, par], slice(0, P), 0, P)
                    store(vnat, slice(0, P), KVW, P, kv_stored[1])
                elif kind == "k":
                    act.wait_ge(kv_stored[par], i * 32 + {11: 32, 12: 32, 15: 96, 16: 96}[c])
                    move(kst[:, par], slice(0, GW), 0, GW).then_inc(turned_out, 1)
                    act.wait_ge(turned_out, g - 9)
                    store(kst[:, par], slice(0, GW), (g - G_K) * GW + P, GW)
                else:
                    col = bass.ds((g - G_V) * GW + P, GW)
                    move(vnat, col, 0, GW).then_inc(turned_out, 1)
                    act.wait_ge(turned_out, g - 9)
                    store(vnat, col, (g - G_V) * GW + (KVW + P), GW)

            def step(g, i, c, kind, turn):
                par, h = c % 2, i + c // 2
                for j in range(4):
                    split(g + 1, j)
                act.wait_ge(chunk_done, g * 4 + 4)
                ps = psM[par]
                if kind in ("q", "k", "kva"):
                    n = 1 if kind == "kva" else 2
                    if c > 0:
                        act.wait_ge(evac[1 - par], i + ((c - 1) // 2 + 1))
                    for q in range(4):
                        last = act.activation(rot[32 * q:32 * q + 32, 0:n], ps[32 * (q ^ 1):32 * (q ^ 1) + 32, 0:n, 0:NTOK],
                                              ACT.Copy)
                    if kind == "kva":
                        last = act.activation(tT[:, par, 1], ps[:, 1, 0:NTOK], ACT.Copy)
                    last.then_inc(rot_ready, 1)
                elif kind == "v":
                    act.wait_ge(turned, g - 11)
                    if c <= 18:
                        act.wait_ge(kcopy, 7 if c == 18 else 6)
                    act.activation(tT[:, par], ps[:, :, 0:NTOK], ACT.Copy).then_inc(evac[par], 1)
                else:
                    if c > 24:
                        act.wait_ge(gate_stored[par], i * 16 + 16)
                    act.activation(gstage[:, par], ps[:, :, 0:NTOK], ACT.Sigmoid).then_inc(evac[par], 1)
                    act.wait_ge(evac[par], h + 1)
                    act.dma_start(gates_d[bass.ds((g - G_G) * 2, 2)].rearrange("t p n -> p t n"), gstage[:, par]
                                  ).then_inc(gate_stored[par], 16)
                if turn:
                    turn_out(g - 1, i, c - 1, turn)

            projections(act, step)

            def o_evac(j, k):
                kind, e, qb = UNITS[k]
                ps = psO[:, k % 2]
                act.wait_ge(pv, j * NU + (k + 1))
                if kind == "B":
                    last = act.activation(oT[64 * e:64 * e + 64, bass.ds(j + 8, 1), P * qb:P * qb + P],
                                          ps[64 * e:64 * e + 64, 0:P].rearrange("p (a n) -> p a n", a=1), ACT.Copy)
                elif kind == "A":
                    last = act.activation(oT[:, bass.ds(j + 4 * e, 1), P * qb:P * qb + P],
                                          ps[:, 0:P].rearrange("p (a n) -> p a n", a=1), ACT.Copy)
                elif kind == "SB":
                    for hh in range(2):
                        src = ps[64 * hh:64 * hh + 64, 0:64].rearrange("p (a c h e) -> p a h e c", a=4, c=4, h=2)[:, :, hh]
                        dst = oT[64 * hh:64 * hh + 64, 8:12, bass.ds(j * 16 + (SEQ + 8 * e), 8)].rearrange("p a (e c) -> p a e c", e=2)
                        last = act.activation(dst, src, ACT.Copy)
                else:
                    for kv in range(2):
                        for w in range(2):
                            src = ps[64 * kv:64 * kv + 64, 64 * kv:64 * kv + 64].rearrange("p (t w i) -> p t w i", t=4, w=2)[:, :, w]
                            dst = oT[64 * w:64 * w + 64, 4 * kv:4 * kv + 4, bass.ds(j * 16 + (SEQ + 8 * e), 8)]
                            last = act.activation(dst, src, ACT.Copy)
                last.then_inc(o_out, 1)

            with act.Fori(0, 4) as j:
                for k, (kind, e, qb) in enumerate(UNITS):
                    par = k % 2
                    s = st[:, par]
                    act.wait_ge(shifted, j * NU + (k + 1))
                    if kind == "A":
                        nk = P * (qb + 1)
                        for hh in range(2):
                            act.activation(S[:, par, hh * nk:hh * nk + nk], S[:, par, hh * nk:hh * nk + nk], ACT.Exp,
                                           bias=s[:, 2 + hh:3 + hh], accum_out=s[:, 4 + hh:5 + hh])
                        act.activation(s[:, 6:8], s[:, 12:14], ACT.Exp).then_inc(exped, 1)
                    else:
                        n = {"B": 384 * (qb + 1), "SB": 576, "SA": 192}[kind]
                        act.activation(S[:, par, 0:n], S[:, par, 0:n], ACT.Exp, bias=s[:, 2:3], accum_out=s[:, 4:5])
                        act.activation(s[:, 6:7], s[:, 12:13], ACT.Exp).then_inc(exped, 1)
                    if k:
                        o_evac(j, k - 1)
                    act.wait_ge(pT, j * NU + (k + 1))
                    if kind == "B":
                        act.activation(PT[:, 0:384 * (qb + 1)], psTf[:, 0:384 * (qb + 1)], ACT.Copy).then_inc(pT_out, 1)
                    elif kind == "A":
                        act.activation(PT[:, 0:256 * (qb + 1)], psTf[:, 0:256 * (qb + 1)], ACT.Copy).then_inc(pT_out, 1)
                    else:
                        n = 384 if kind == "SB" else P
                        act.activation(PT[:, 0:n], psTf[:, 0:n], ACT.Copy)
                        act.activation(PT[0:64, 384:384 + n], psTf[0:64, 384:384 + n], ACT.Copy).then_inc(pT_out, 1)
                o_evac(j, NU - 1)

            act.wait_ge(o_out, 4 * NU)
            for j in range(3):
                act.activation(ohi[:, 4 * j:4 * j + 4], oT[:, 4 * j:4 * j + 4], ACT.Copy).then_inc(o_hi, 1)

            with act.Fori(0, 2) as i:
                for q in range(4):
                    for j in range(3):
                        s = 3 * q + j
                        split(i * 3 + (C_BR // 4 + 1 + s // 4), s % 4)
                    act.wait_ge(m_sum, i * 4 + (q + 1))
                    act.activation(mhi[:, bass.ds(i * 8 + 2 * q, 2)], t2[:, q % 2], ACT.Copy).then_inc(m_hi, 1)

            with act.Fori(0, 8) as i:
                for j in range(4):
                    split(i + (C_WO // 4 + 1), j)

            def layer_norm(li, gam, bet):
                for half in range(2):
                    act.wait_ge(ln_dve, 30 * li + 2 + half)
                    act.activation(gt[:, :, :].rearrange("p a b n -> p (a b) n"), r[:, 8 * half:8 * half + 8], ACT.Square
                                   ).then_inc(ln_act, 1)
                act.wait_ge(ln_dve, 30 * li + 6)
                act.activation(lnrow[:, 0], lnrow[:, 0], ACT.Sqrt).then_inc(ln_act, 1)
                for j in range(4):
                    act.wait_ge(ln_dve, 30 * li + 8 + j)
                    for t in range(4 * j, 4 * j + 4):
                        last = act.activation(r[:, t], r[:, t], ACT.Identity, bias=bet[:, t:t + 1], scale=gam[:, t:t + 1])
                    last.then_inc(ln_act, 1)
                    act.wait_ge(ln_act, 7 * li + 4 + j)
                    if li == 0:
                        act.activation(hhi[:, 4 * j:4 * j + 4], r[:, 4 * j:4 * j + 4], ACT.Copy).then_inc(h_hi, 1)
                    else:
                        act.dma_start(o["yT"].rearrange("(t p) n -> p t n", p=P)[:, 4 * j:4 * j + 4],
                                      r[:, 4 * j:4 * j + 4]).then_inc(y_out, 16)

            layer_norm(0, ln1g, ln1b)

            def up(b, q, c):
                par = 1 - c
                for j in range(4):
                    split(b * 16 + q * 2 + (C_FF // 4 + 1 + c), j)
                act.wait_ge(chunk_done, b * C_BLK + q * 8 + (C_FF + 4 * c + 4))
                for t in range(2):
                    last = act.activation(t2[:, c, t], psM[par][:, t, 0:NTOK], ACT.Relu,
                                          bias=bff1[:, bass.ds(b * 16 + q * 4 + (2 * c + t), 1)])
                last.then_inc(evac[par], 1)
                act.wait_ge(u_done, b * 8 + q * 2 + (c + 1))
                act.activation(uhi[:, bass.ds(q * 4 + 2 * c, 2)], t2[:, c], ACT.Copy).then_inc(u_hi, 1)

            with act.Fori(0, 3) as b:
                with act.Fori(0, 4) as q:
                    up(b, q, 0)
                    up(b, q, 1)
                with act.Fori(0, 8) as q:
                    for j in range(4):
                        split(b * 16 + q + (C_FF // 4 + 9), j)
            with act.Fori(0, 4) as q:
                up(3, q, 0)
                up(3, q, 1)
            with act.Fori(0, 7) as q:
                for j in range(4):
                    split(q + (3 * 16 + C_FF // 4 + 9), j)
            layer_norm(1, ln2g, ln2b)

        @block.vector
        def _(dve):
            def split(q, slot, first=False):
                dve.wait_ge(hi_done, q * 4 + (slot + 1))
                if not first:
                    dve.wait_ge(chunk_done, q * 4 + (slot - RING + 1))
                dve.tensor_tensor(wlo[:, slot], raw[:, slot], whi[:, slot].bitcast(F32), ALU.subtract).then_inc(lo_done, 1)

            for j in range(4):
                dve.wait_ge(x_hi, j + 1)
                dve.tensor_tensor(xlo[:, 4 * j:4 * j + 4], xraw[:, 4 * j:4 * j + 4],
                                  xhi[:, 4 * j:4 * j + 4].bitcast(F32), ALU.subtract).then_inc(x_lo, 1)
                split(0, j, first=True)
            dve.wait_ge(const_in, 16 * 8)

            def step(g, i, c, kind, turn):
                par, h = c % 2, i + c // 2
                for j in range(4):
                    split(g + 1, j)
                if kind in ("v", "gate"):
                    return
                n = 1 if kind == "kva" else 2
                dst = {"q": lambda: qT[:, bass.ds(g * 2, 2)],
                       "k": lambda: tT[:, par], "kva": lambda: tT[:, par, 0:1]}[kind]()
                cos, sin = (rope[:, k:k + 1].broadcast_to([P, n, NTOK]) for k in range(2))
                dve.wait_ge(chunk_done, g * 4 + 4)
                if kind == "k" and c > 11:
                    dve.wait_ge(turned, g - 11)
                    dve.wait_ge(kcopy, g - 11)
                dve.wait_ge(rot_ready, g + 1)
                dve.tensor_tensor(dst, psM[par][:, 0:n, 0:NTOK], cos, ALU.mult).then_inc(rope_a, 1)
                dve.tensor_tensor(rot[:, 0:n], rot[:, 0:n], sin, ALU.mult).then_inc(rope_b, 1)
                dve.wait_ge(rope_a, g + 1)
                dve.wait_ge(rope_b, g + 1)
                dve.tensor_tensor(dst, dst, rot[:, 0:n], ALU.add).then_inc(evac[par], 1)
                if kind == "kva":
                    dve.wait_ge(evac[par], h + 1)
                    src = tT[:, par, 0]
                    dve.tensor_copy(kTa[:, 0], src)
                    for kv in range(2):
                        for half in range(2):
                            last = dve.tensor_copy(kTa[64 * half:64 * half + 64, 1 + kv], src[64 * kv:64 * kv + 64])
                    last.then_inc(kcopy, 1)

            projections(dve, step)

            dve.wait_ge(turned_out, 13)
            dve.wait_ge(kcopy, 7)
            dve.wait_ge(kv_stored[0], 16 * 14)
            dve.wait_ge(kv_stored[1], 16 * 14)
            dve.wait_ge(gate_stored[0], 16 * 8)
            dve.wait_ge(gate_stored[1], 16 * 8)
            dve.memset(QbS[:], 0.0)
            dve.memset(QaS[:], 0.0).then_inc(zeroed, 1)
            dve.wait_ge(zeroed, 2)

            def stage(j, k):
                kind, e, qb = UNITS[k]
                if k == 0:
                    q4, k4 = (t.rearrange("p (g a) n -> p g a n", g=3) for t in (qTb, kTb[:, :, :]))
                    dve.tensor_copy(QB[:], q4[:, :, bass.ds(j, 1), 0:256].rearrange("p g a n -> p g (a n)"))
                    dve.tensor_copy(KB[:], k4[:, :, bass.ds(j, 1), 0:256].rearrange("p g a n -> p g (a n)"))
                    for kb in range(2):
                        dve.tensor_copy(VB[:, kb], vnat[:, kb, P:KVW].rearrange("p (g n) -> p g n", g=3)[:, :, bass.ds(j * P, P)])
                    q2 = qTa.rearrange("p (a b) n -> p a b n", a=2)
                    dve.tensor_copy(QA[:], q2[:, :, bass.ds(j, 1), 0:256].rearrange("p a b n -> p a (b n)")).then_inc(staged, 1)
                elif kind == "SB":
                    for g in range(3):
                        for hh in range(2):
                            src = qTb[64 * hh:64 * hh + 64, 4 * g:4 * g + 4, bass.ds(j * 16 + (SEQ + 8 * e), 8)].rearrange("p a (e c) -> p a c e", e=2)
                            for pr in range(4):
                                dst = QbS[64 * hh:64 * hh + 64, g, pr].rearrange("p (c w) -> p c w", c=4)[:, :, 4 * pr + 2 * hh:4 * pr + 2 * hh + 2]
                                last = dve.tensor_copy(dst, src[:, pr])
                    last.then_inc(staged, 1)
                elif kind == "SA":
                    for kv in range(2):
                        for w in range(2):
                            dst = QaS[64 * kv:64 * kv + 64, 64 * kv:64 * kv + 64].rearrange("p (t w i) -> p t w i", t=4, w=2)[:, :, w]
                            src = qTa[64 * w:64 * w + 64, 4 * kv:4 * kv + 4, bass.ds(j * 16 + (SEQ + 8 * e), 8)]
                            last = dve.tensor_copy(dst, src)
                    last.then_inc(staged, 1)

            with dve.Fori(0, 4) as j:
                stage(j, 0)
                for k, (kind, e, qb) in enumerate(UNITS):
                    par, U1 = k % 2, j * NU + (k + 1)
                    if k + 1 < NU:
                        stage(j, k + 1)
                    ps = psM[par][:, :, :].rearrange("p a (b n) -> p (a b) n", b=2)
                    s, Sp = st[:, par], S[:, par]
                    nk = P * (qb + 1)
                    pm = mask_p[:, :, P * qb:P * qb + nk]
                    dve.wait_ge(scores, U1)
                    if k >= 2:
                        dve.wait_ge(pT, j * NU + (k - 1))
                    if kind == "B":
                        nh, n = 1, 3 * nk
                        dve.scalar_tensor_tensor(Sp[:, 0:n].rearrange("p (g k) -> p g k", g=3), ps[:, 0:3, 0:nk], SCALE, pm,
                                                 ALU.mult, ALU.add).then_inc(masked, 1)
                    elif kind == "A":
                        nh, n = 2, nk
                        for hh in range(2):
                            last = dve.scalar_tensor_tensor(Sp[:, hh * nk:hh * nk + nk], ps[:, 2 * hh, 0:nk], SCALE, pm[:, 0], ALU.mult, ALU.add)
                        last.then_inc(masked, 1)
                    else:
                        b0, nb = (0, 3) if kind == "SB" else (3, 1)
                        nh, n = 1, 192 * nb
                        Sv = Sp[:, 0:n].rearrange("p (g k) -> p g k", g=nb)
                        dve.scalar_tensor_tensor(Sv[:, :, 0:P], ps[:, 0:nb, 0:P], SCALE, mask_c[:, b0:b0 + nb], ALU.mult, ALU.add)
                        win = bass.ds(j * (-16) + (56 - 8 * e), 64)
                        dve.scalar_tensor_tensor(Sv[:, :, P:192], ps[:, 0:nb, P:192], SCALE, mask_n[:, b0:b0 + nb, win],
                                                 ALU.mult, ALU.add).then_inc(masked, 1)
                    dve.wait_ge(masked, U1)
                    dve.tensor_reduce(s[:, 0:nh], Sp[:, 0:nh * n].rearrange("p (h k) -> p h k", h=nh), AX.X, ALU.max).then_inc(maxed, 1)
                    if kind == "A":
                        sink = sink_p[:, bass.ds(j * 2 + 8 * e, 2)]
                    else:
                        sink = sink_s[:, 0:1] if kind == "SA" else sink_s[:, 1:2]
                    dve.wait_ge(maxed, U1)
                    dve.tensor_tensor(s[:, 0:nh], s[:, 0:nh], sink, ALU.max).then_inc(sinkmax, 1)
                    dve.wait_ge(sinkmax, U1)
                    dve.tensor_scalar(s[:, 2:2 + nh], s[:, 0:nh], -1.0, None, ALU.mult)
                    dve.tensor_tensor(s[:, 12:12 + nh], sink, s[:, 0:nh], ALU.subtract).then_inc(shifted, 1)
                    dve.wait_ge(exped, U1)
                    dve.tensor_tensor(s[:, 8:8 + nh], s[:, 4:4 + nh], s[:, 6:6 + nh], ALU.add).then_inc(denom, 1)
                    dve.wait_ge(denom, U1)
                    dve.reciprocal(s[:, 10:10 + nh], s[:, 8:8 + nh]).then_inc(recip, 1)
                    dve.wait_ge(recip, U1)
                    for hh in range(nh):
                        last = dve.tensor_scalar(Sp[:, hh * n:hh * n + n], Sp[:, hh * n:hh * n + n], s[:, 10 + hh:11 + hh], None, ALU.mult)
                    last.then_inc(normed, 1)

            for j in range(3):
                dve.wait_ge(o_hi, j + 1)
                dve.tensor_tensor(olo[:, 4 * j:4 * j + 4], oT[:, 4 * j:4 * j + 4], ohi[:, 4 * j:4 * j + 4].bitcast(F32),
                                  ALU.subtract).then_inc(o_lo, 1)

            with dve.Fori(0, 2) as i:
                for q in range(4):
                    c0 = C_BR + 3 * q
                    for j in range(2):
                        s = 3 * q + j
                        split(i * 3 + (C_BR // 4 + 1 + s // 4), s % 4)
                    dve.wait_ge(chunk_done, i * 12 + (c0 + 2))
                    dve.wait_ge(g_in[2 * (q % 2)], i * 32 + 16 * (q // 2 + 1))
                    dve.tensor_tensor(t1[:], psM[1][:, :, 0:NTOK], gt[:, 2 * (q % 2)], ALU.mult).then_inc(evac[1], 1)
                    s = 3 * q + 2
                    split(i * 3 + (C_BR // 4 + 1 + s // 4), s % 4)
                    dve.wait_ge(chunk_done, i * 12 + (c0 + 3))
                    dve.wait_ge(g_in[2 * (q % 2) + 1], i * 32 + 16 * (q // 2 + 1))
                    dve.tensor_tensor(t2[:, q % 2], psM[0][:, :, 0:NTOK], gt[:, 2 * (q % 2) + 1], ALU.mult).then_inc(evac[0], 1)
                    dve.wait_ge(evac[1], i * 4 + (q + G_BR // 2 + 1))
                    dve.wait_ge(evac[0], i * 4 + (q + (G_BR + 1) // 2 + 1))
                    dve.tensor_tensor(t2[:, q % 2], t1[:], t2[:, q % 2], ALU.add).then_inc(m_sum, 1)
                    dve.wait_ge(m_hi, i * 4 + (q + 1))
                    dve.tensor_tensor(mlo[:, bass.ds(i * 8 + 2 * q, 2)], t2[:, q % 2], mhi[:, bass.ds(i * 8 + 2 * q, 2)].bitcast(F32),
                                      ALU.subtract).then_inc(m_lo, 1)

            with dve.Fori(0, 4) as i:
                for c in range(2):
                    for j in range(4):
                        split(i * 2 + (C_WO // 4 + 1 + c), j)
                    dve.wait_ge(chunk_done, i * 8 + (C_WO + 4 * c + 4))
                    dve.wait_ge(xr_in[c], i * 16 + 16)
                    dve.scalar_tensor_tensor(r[:, bass.ds(i * 4 + 2 * c, 2)], xres[:, c], ALPHA, psM[1 - c][:, :, 0:NTOK],
                                             ALU.mult, ALU.add).then_inc(evac[1 - c], 1)

            def layer_norm(li):
                base = 30 * li
                row = [lnrow[:, k] for k in range(3)]
                g8 = gt[:, :, :].rearrange("p a b n -> p n (a b)")
                dve.tensor_reduce(row[0], r[:, :, :].rearrange("p t n -> p n t"), AX.X, ALU.add).then_inc(ln_dve, 1)
                dve.wait_ge(ln_pe, 2 * li + 1)
                dve.tensor_tensor(r[:], r[:], psT[:, 0:1, 0:NTOK].broadcast_to([P, 16, NTOK]), ALU.subtract).then_inc(ln_dve, 1)
                dve.wait_ge(ln_act, 7 * li + 1)
                dve.tensor_reduce(row[1], g8, AX.X, ALU.add).then_inc(ln_dve, 1)
                dve.wait_ge(ln_act, 7 * li + 2)
                dve.tensor_reduce(row[2], g8, AX.X, ALU.add).then_inc(ln_dve, 1)
                dve.wait_ge(ln_dve, base + 4)
                dve.tensor_tensor(row[1], row[1], row[2], ALU.add).then_inc(ln_dve, 1)
                dve.wait_ge(ln_pe, 2 * li + 2)
                dve.tensor_scalar(row[0], psT[:, 1, 0:NTOK], EPS, None, ALU.add).then_inc(ln_dve, 1)
                dve.wait_ge(ln_act, 7 * li + 3)
                dve.reciprocal(row[1], row[0]).then_inc(ln_dve, 1)
                dve.wait_ge(ln_dve, base + 7)
                for j in range(4):
                    part = r[:, 4 * j:4 * j + 4]
                    dve.tensor_tensor(part, part, lnrow[:, 1:2].broadcast_to([P, 4, NTOK]), ALU.mult).then_inc(ln_dve, 1)

            dve.wait_ge(evac[1], G_FF // 2 + 0)
            dve.wait_ge(evac[0], G_FF // 2 + 1)
            layer_norm(0)
            for j in range(4):
                dve.wait_ge(h_hi, j + 1)
                dve.tensor_tensor(hlo[:, 4 * j:4 * j + 4], r[:, 4 * j:4 * j + 4], hhi[:, 4 * j:4 * j + 4].bitcast(F32),
                                  ALU.subtract).then_inc(h_lo, 1)
            dve.wait_ge(h_lo, 4)
            for t in range(16):
                last = dve.tensor_scalar(r[:, t], r[:, t], ALPHA, bff2[:, t:t + 1], ALU.mult, ALU.add)
            last.then_inc(ln_dve, 30 - 11)
            dve.wait_ge(ln_dve, 30)

            def up(b, q, c):
                for j in range(4):
                    split(b * 16 + q * 2 + (C_FF // 4 + 1 + c), j)
                dve.wait_ge(evac[1 - c], b * 8 + q + ((G_FF + c) // 2 + 1))
                dve.tensor_tensor(t2[:, c], t2[:, c], t2[:, c], ALU.mult).then_inc(u_done, 1)
                dve.wait_ge(u_hi, b * 8 + q * 2 + (c + 1))
                part = bass.ds(q * 4 + 2 * c, 2)
                dve.tensor_tensor(ulo[:, part], t2[:, c], uhi[:, part].bitcast(F32), ALU.subtract).then_inc(u_lo, 1)

            def down(b, q, c, last=False):
                if not last:
                    for j in range(4):
                        split(b * 16 + q * 2 + (C_FF // 4 + 9 + c), j)
                dve.wait_ge(chunk_done, b * C_BLK + q * 8 + (C_FF + 32 + 4 * c + 4))
                part = r[:, bass.ds(q * 4 + 2 * c, 2)]
                dve.tensor_tensor(part, part, psM[1 - c][:, :, 0:NTOK], ALU.add).then_inc(evac[1 - c], 1)

            with dve.Fori(0, 3) as b:
                with dve.Fori(0, 4) as q:
                    up(b, q, 0)
                    up(b, q, 1)
                with dve.Fori(0, 4) as q:
                    down(b, q, 0)
                    down(b, q, 1)
            with dve.Fori(0, 4) as q:
                up(3, q, 0)
                up(3, q, 1)
            with dve.Fori(0, 3) as q:
                down(3, q, 0)
                down(3, q, 1)
            down(3, 3, 0)
            down(3, 3, 1, last=True)
            dve.wait_ge(evac[1], (G_FF + 64) // 2)
            dve.wait_ge(evac[0], (G_FF + 65) // 2)
            layer_norm(1)

        @block.tensor
        def _(pe):
            def chunk(c, slot, ps, hi, lo, t0, first, last):
                pe.wait_ge(lo_done, c + 1)
                for k in range(KT):
                    for t in range(2):
                        wh, wl = (w[:, slot, k, P * t:P * t + P] for w in (whi, wlo))
                        out = ps[:, t, 0:NTOK]
                        pe.matmul(out, wh, hi[:, t0 + k], start=first and k == 0, stop=False)
                        pe.matmul(out, wh, lo[:, t0 + k], start=False, stop=False)
                        mm = pe.matmul(out, wl, hi[:, t0 + k], start=False, stop=last and k == KT - 1)
                mm.then_inc(chunk_done, 1)

            def group(c, ps, hi, lo, ready=None):
                for j in range(4):
                    if ready is not None:
                        pe.wait_ge(*ready(j))
                    chunk(c + j, j, ps, hi, lo, 4 * j, j == 0, j == 3)

            def turn(g, i, c):
                par = c % 2
                pe.wait_ge(evac[par], i + (c // 2 + 1))
                if c > 10:
                    pe.wait_ge(turned_out, g - 10)
                for k in range(3):
                    n = P if k < 2 else 64
                    for t in range(2):
                        mm = pe.transpose(psTf[0:n, k * GW + t * P:k * GW + t * P + P], tT[:, par, t, k * P:k * P + n], ident[:])
                mm.then_inc(turned, 1)

            def step(g, i, c, kind, turned_kind):
                par, h = c % 2, i + c // 2
                if c >= 2:
                    pe.wait_ge(evac[par], h)
                if c == 0:
                    group(g * 4, psM[par], xhi, xlo, ready=lambda j: (x_lo, j + 1))
                else:
                    group(g * 4, psM[par], xhi, xlo)
                if turned_kind:
                    if c == 11:
                        pe.wait_ge(const_in, 16 * 8)
                    turn(g - 1, i, c - 1)

            projections(pe, step)

            def unit_scores(j, k):
                kind, e, qb = UNITS[k]
                ps = psM[k % 2][:, :, :].rearrange("p a (b n) -> p (a b) n", b=2)
                if k in STAGED:
                    pe.wait_ge(staged, j * 5 + STAGED[k])
                if k >= 2:
                    pe.wait_ge(masked, j * NU + (k - 1))
                nk, qs = P * (qb + 1), slice(P * qb, P * qb + P)
                if kind == "B":
                    for g in range(3):
                        mm = pe.matmul(ps[:, g, 0:nk], QB[64 * e:64 * e + 64, g, qs], KB[64 * e:64 * e + 64, g, 0:nk],
                                       start=True, stop=True)
                elif kind == "A":
                    for hh in range(2):
                        mm = pe.matmul(ps[:, 2 * hh, 0:nk], QA[64 * hh:64 * hh + 64, e, qs], kTa[64 * hh:64 * hh + 64, 1 + e, 0:nk],
                                       start=True, stop=True)
                elif kind == "SB":
                    pe.wait_ge(kc_in, j * 64 + 32 * (e + 1))
                    for pr in range(4):
                        mm = pe.matmul(ps[:, 0, 0:P], QbS[:, 0, pr], kcache[:, pr, 0], start=pr == 0, stop=pr == 3)
                    for g in range(1, 3):
                        for pr in range(4):
                            for c in range(4):
                                mm = pe.matmul(ps[32 * c:32 * c + 32, g, 0:P], QbS[:, g, pr, 32 * c:32 * c + 32],
                                               kcache[:, pr, 1 + 4 * (g - 1) + c], start=pr == 0, stop=pr == 3)
                    for g in range(3):
                        for pr in range(4):
                            mm = pe.matmul(ps[:, g, P:192], QbS[:, g, pr], kTb[:, 4 * g + pr, SEQ:NTOK], start=pr == 0, stop=pr == 3)
                else:
                    pe.matmul(ps[:, 0, 0:P], QaS[:], kca[:], start=True, stop=True)
                    mm = pe.matmul(ps[:, 0, P:192], QaS[:], kTa[:, 0, SEQ:NTOK], start=True, stop=True)
                mm.then_inc(scores, 1)

            def unit_values(j, k):
                kind, e, qb = UNITS[k]
                Sp, out, nk = S[:, k % 2], psO[:, k % 2], P * (qb + 1)
                pe.wait_ge(normed, j * NU + (k + 1))
                if kind in ("A", "B"):
                    nb = (3 if kind == "B" else 2) * (qb + 1)
                    for t in range(nb):
                        mm = pe.transpose(psTf[:, t * P:t * P + P], Sp[:, t * P:t * P + P], ident[:])
                else:
                    nb = 3 if kind == "SB" else 1
                    for g in range(nb):
                        pe.transpose(psTf[:, g * P:g * P + P], Sp[:, 192 * g:192 * g + P], ident[:])
                        mm = pe.transpose(psTf[0:64, 384 + g * P:384 + g * P + P], Sp[:, 192 * g + P:192 * g + 192], ident[:])
                mm.then_inc(pT, 1)
                if kind in ("SB", "SA"):
                    pe.wait_ge(vc_in, j * 64 + 32 * (e + 1))
                pe.wait_ge(pT_out, j * NU + (k + 1))
                if kind == "B":
                    for t in range(nb):
                        g, kb = divmod(t, qb + 1)
                        mm = pe.matmul(out[64 * e:64 * e + 64, 0:P], VB[:, kb, g, 64 * e:64 * e + 64], PT[:, t * P:t * P + P],
                                       start=t == 0, stop=t == nb - 1)
                elif kind == "A":
                    for hh in range(2):
                        for kb in range(qb + 1):
                            t = hh * (qb + 1) + kb
                            mm = pe.matmul(out[64 * hh:64 * hh + 64, 0:P], vnat[:, kb, 64 * e:64 * e + 64], PT[:, t * P:t * P + P],
                                           start=kb == 0, stop=kb == qb)
                elif kind == "SB":
                    PTv = PT[:, 0:768].rearrange("p (g c w) -> p g c w", g=6, c=4)
                    for pr in range(4):
                        o16, w = out[:, 16 * pr:16 * pr + 16].rearrange("p (c w) -> p c w", c=4), slice(4 * pr, 4 * pr + 4)
                        ch = slice(P * pr, P * pr + P)
                        pe.matmul(o16, vcache[:, 0, ch], PTv[:, 0, :, w], start=pr == 0, stop=False, skip_group_check=True)
                        for g in range(1, 3):
                            for c in range(4):
                                pe.matmul(o16[:, c], vcache[:, 1 + 4 * (g - 1) + c, ch], PTv[:, g, c, w], start=False, stop=False,
                                          skip_group_check=True)
                        for g in range(3):
                            mm = pe.matmul(o16, vnat[0:64, 2, P + 512 * g + P * pr:P + 512 * g + P * pr + P], PTv[0:64, 3 + g, :, w],
                                           start=False, stop=g == 2, skip_group_check=True)
                else:
                    pe.matmul(out[:, 0:P], vca[:], PT[:, 0:P], start=True, stop=False)
                    mm = pe.matmul(out[:, 0:P], vnat[0:64, 2, 0:P], PT[0:64, 384:512], start=False, stop=True)
                mm.then_inc(pv, 1)

            pe.wait_ge(evac[0], G_BR // 2 + 1)
            pe.wait_ge(evac[1], G_BR // 2)
            with pe.Fori(0, 4) as j:
                unit_scores(j, 0)
                for k in range(NU):
                    if k + 1 < NU:
                        unit_scores(j, k + 1)
                    unit_values(j, k)

            with pe.Fori(0, 2) as i:
                for q in range(4):
                    s = 3 * q
                    pe.wait_ge(evac[1], i * 4 + (q + G_BR // 2))
                    for j in range(2):
                        pe.wait_ge(o_lo, j + 1)
                        chunk(i * 12 + (C_BR + s + j), (s + j) % 4, psM[1], ohi, olo, 4 * j, j == 0, j == 1)
                    pe.wait_ge(evac[0], i * 4 + (q + G_BR // 2 + 1))
                    pe.wait_ge(o_lo, 3)
                    chunk(i * 12 + (C_BR + s + 2), (s + 2) % 4, psM[0], ohi, olo, 8, True, True)

            with pe.Fori(0, 4) as i:
                for c in range(2):
                    pe.wait_ge(evac[1 - c], i + ((G_WO + c) // 2))
                    group(i * 8 + (C_WO + 4 * c), psM[1 - c], mhi, mlo, ready=lambda j: (m_lo, 2 * j + 2))

            def layer_norm(li):
                pe.wait_ge(ln_dve, 30 * li + 1)
                pe.matmul(psT[:, 0, 0:NTOK], onesD[:], lnrow[:, 0], start=True, stop=True).then_inc(ln_pe, 1)
                pe.wait_ge(ln_dve, 30 * li + 5)
                pe.matmul(psT[:, 1, 0:NTOK], onesD[:], lnrow[:, 1], start=True, stop=True).then_inc(ln_pe, 1)

            layer_norm(0)

            with pe.Fori(0, 4) as b:
                with pe.Fori(0, 4) as q:
                    for c in range(2):
                        pe.wait_ge(evac[1 - c], b * 8 + q + ((G_FF + c) // 2))
                        group(b * C_BLK + q * 8 + (C_FF + 4 * c), psM[1 - c], hhi, hlo, ready=lambda j: (h_lo, j + 1))
                with pe.Fori(0, 4) as q:
                    for c in range(2):
                        pe.wait_ge(evac[1 - c], b * 8 + q + ((G_FF + 8 + c) // 2))
                        group(b * C_BLK + q * 8 + (C_FF + 32 + 4 * c), psM[1 - c], uhi, ulo,
                              ready=lambda j: (u_lo, b * 8 + (2 * j + 2)))
            layer_norm(1)


_CACHES = ["cache_a_kv", "cache_b1_kv", "cache_b2_kv", "cache_b3_kv"]
_WEIGHTS = ["w_in", "w_branch_a", "w_branch_b", "w_out", "w_ff1", "w_ff2"]
_OUTS = {
    "yT": (D, NTOK),
    "a_p": (1, 1, 128, 2, 2, HD), "a_s": (1, DB, 128, 2, 2, HD),
    "b1_p": (1, 1, 128, 2, 8, HD), "b1_s": (1, DB, 128, 2, 8, HD),
    "b2_p": (1, 1, 256, 2, 8, HD), "b2_s": (1, DB, 512, 2, 8, HD),
    "b3_p": (1, 1, 256, 2, 8, HD), "b3_s": (1, DB, 1032, 2, 8, HD),
}


def constants():
    half = HD // 2
    inv = (1.0 / (np.float32(THETA) ** (np.arange(half, dtype=np.float32) / np.float32(half)))).astype(np.float32)
    pos = np.concatenate([np.arange(SEQ), np.tile(PAST + np.arange(DT), DB)]).astype(np.float32)
    ang = (pos[None, :] * inv[:, None]).astype(np.float32)
    cos, sin = np.cos(ang.astype(np.float64)), np.sin(ang.astype(np.float64))
    rope = np.stack([np.tile(cos, (4, 1)), np.tile(np.concatenate([-sin, sin]), (2, 1))], 1).astype(np.float32)

    mask_p = np.full((P, NG, 384), NEG, np.float32)
    q, s = np.arange(P)[:, None], np.arange(256)[None, :]
    for g, dil in enumerate(DIL):
        for qb in range(2):
            dist = P * qb + q - s[:, :P * (qb + 1)]
            ok = (dist >= 0) & (dist % dil == 0) & (dist < 128 * dil)
            mask_p[:, g, P * qb:P * qb + P * (qb + 1)] = np.where(ok, 0, NEG)

    mask_c = np.full((P, 4, P), NEG, np.float32)
    mask_n = np.full((P, 4, 120), NEG, np.float32)
    key = np.arange(P)
    for row in range(P):
        c, w = divmod(row, 32)
        if w < 16:
            i = c + 4 * (w % 2)
            mask_c[row, 0] = np.where(P + i - key < 128, 0, NEG)
            mask_c[row, 1] = np.where(512 + i - (4 * key + c) < 512, 0, NEG)
            mask_c[row, 2] = np.where(4 * (key % 2) + c == i, 0, NEG)
            for g, dil in enumerate(DIL):
                for t in range(DT):
                    if t <= i and (i - t) % dil == 0:
                        mask_n[row, g, 56 + t] = 0
        i = row % 8
        mask_c[row, 3] = np.where(P + i - key < 128, 0, NEG)
        mask_n[row, 3, 56:57 + i] = 0
    return {"rope": rope, "ident": np.eye(P, dtype=np.float32), "mask_p": mask_p, "mask_c": mask_c, "mask_n": mask_n}


def layouts(inputs):
    c = np.ascontiguousarray
    tiles = lambda v: v.reshape(-1, P).T
    x = np.concatenate([inputs["x_prompt"].reshape(SEQ, D), inputs["x_sample"].reshape(DB * DT, D)])
    ka, k1, k2, k3 = (inputs[n][0, :, :, 0] for n in _CACHES)
    va, v1, v2, v3 = (inputs[n][0, :, :, 1] for n in _CACHES)

    def chunks(t1, t2, t3):
        t3 = t3.reshape(DB, 64, 4, 4, H_B, HD)[:, :, 0:2].reshape(DB, P, 4, H_B, HD)
        return np.concatenate([t1[:, :, None], t2.reshape(DB, P, 4, H_B, HD), t3], 2)

    kT_b = chunks(k1, k2, k3).reshape(DB, P, CK, 4, P).transpose(0, 4, 3, 2, 1)
    sinks = inputs["a_sinks"].reshape(QH_A)
    sink_s = np.stack([np.repeat(sinks, DT), np.full(P, NEG, np.float32)], 1)
    out = {
        "xT": c(x.T), "kT_b": c(kT_b).reshape(DB, P, 4 * CK * P), "v_b": chunks(v1, v2, v3).reshape(DB, P, CK * 512),
        "kT_a": c(ka.reshape(DB, P, P).transpose(0, 2, 1)), "v_a": c(va).reshape(DB, P, P),
        "sink_p": c(np.broadcast_to(sinks, (P, QH_A))), "sink_s": c(sink_s),
        "vecs": c(np.concatenate([tiles(inputs[n][0]) for n in ("ln1_g", "ln1_b", "ln2_g", "ln2_b", "b_ff2", "b_ff1")], 1)),
    }
    out.update({n: c(inputs[n]) for n in _CACHES + _WEIGHTS})
    return out


def kernel(**inputs):
    import concourse.bacc as _bacc
    from concourse.bass_utils import run_bass_kernel_spmd as _run

    inputs = {n: np.asarray(v) for n, v in inputs.items()}
    nc = _bacc.Bacc("TRN2", target_bir_lowering=False, num_devices=1)
    arrays, ins, outs = {}, {}, {}
    for name, v in {**layouts(inputs), **constants()}.items():
        arrays[f"in_{name}_dram"] = v
        ins[name] = nc.dram_tensor(f"in_{name}_dram", v.shape, mybir.dt.from_np(v.dtype), kind="ExternalInput").ap()
    for name, shape in _OUTS.items():
        outs[name] = nc.dram_tensor(f"out_{name}_dram", shape, F32, kind="ExternalOutput").ap()
    program(nc, ins, outs)
    got = _run(nc, [arrays], core_ids=[0]).results[0]
    g = {name: got[f"out_{name}_dram"] for name in _OUTS}
    y = np.ascontiguousarray(g["yT"].T)
    return (y[:SEQ].reshape(1, SEQ, D), y[SEQ:].reshape(DB, DT, D), g["a_p"], g["a_s"], g["b1_p"], g["b1_s"],
            g["b2_p"], g["b2_s"], g["b3_p"], g["b3_s"])
```

```python
from contextlib import ExitStack

import concourse.bass as bass
import numpy as np
from concourse import mybir

F32 = mybir.dt.float32
F32R = mybir.dt.float32r
ACT = mybir.ActivationFunctionType
ALU = mybir.AluOpType
AX = mybir.AxisListType

P = 128
D = 2048
DFF = 4 * D
SEQ, DB, DT, PAST = 256, 8, 8, 1024
NTOK = SEQ + DB * DT
HD = 64
QH_A, KV_A, H_B, NG = 16, 2, 8, 3
GW = 256
KT = 4
RING = 4
NEG = -1e30
SCALE = HD ** -0.5
ALPHA = 2.0 ** 0.25
EPS = 1e-5
THETA = 10000.0
WIN = (128, 512, 2048)
DIL = (1, 4, 16)
KVW = 1664
CK = 9


def program(nc, a, o):
    ctx = ExitStack()
    with ctx:
        def sb(name, shape, dt=F32):
            return ctx.enter_context(nc.sbuf_tensor("s_" + name, shape, dt))

        def sem(name):
            return ctx.enter_context(nc.semaphore(name))

        raw = sb("raw", [P, RING, KT, GW])
        whi = sb("whi", [P, RING, KT, GW], F32R)
        wlo = sb("wlo", [P, RING, KT, GW], F32R)

        def overlay(*sets):
            made, base = [], []
            for k, tensors in enumerate(sets):
                with ExitStack() as own:
                    made.append([own.enter_context(nc.sbuf_tensor("s_" + n, s, d)) for n, s, d in tensors])
            size = [sum(int(np.prod(s[1:])) for _, s, _ in t) for t in sets]
            ctx.enter_context(nc.sbuf_tensor(f"hold_{len(made)}_{sets[0][0][0]}", [P, max(size)], F32))
            return made

        (xhi, xlo), (kcache, vcache, onat), (ohi, olo), (hhi, hlo) = overlay(
            [("xhi", [P, 16, NTOK], F32R), ("xlo", [P, 16, NTOK], F32R)],
            [("kcache", [P, 4, CK, P], F32), ("vcache", [P, CK, 512], F32),
             ("onat", [P, 512], F32)],
            [("ohi", [P, 12, NTOK], F32R), ("olo", [P, 12, NTOK], F32R)],
            [("hhi", [P, 16, NTOK], F32R), ("hlo", [P, 16, NTOK], F32R)],
        )
        (xraw,), (vnat, qT, kTb, kTa), (r, mhi, mlo), (_, uhi, ulo) = overlay(
            [("xraw", [P, 16, NTOK], F32)],
            [("vnat", [P, 3, KVW], F32), ("qT", [P, 20, NTOK], F32),
             ("kTb", [P, 12, NTOK], F32), ("kTa", [P, 3, NTOK], F32)],
            [("r", [P, 16, NTOK], F32), ("mhi", [P, 16, NTOK], F32R), ("mlo", [P, 16, NTOK], F32R)],
            [("r_again", [P, 16, NTOK], F32), ("uhi", [P, 16, NTOK], F32R), ("ulo", [P, 16, NTOK], F32R)],
        )
        (tT, rot, kst, gstage, rope), (QB, KB, VB, QA, QbS, QaS, kca, vca, S, PT), (gt, xres, t1, t2, lnrow) = overlay(
            [("tT", [P, 2, 2, NTOK], F32), ("rot", [P, 2, NTOK], F32), ("kst", [P, 2, 3, GW], F32),
             ("gstage", [P, 2, 2, NTOK], F32), ("rope", [P, 2, NTOK], F32)],
            [("QB", [P, 3, 256], F32), ("KB", [P, 3, 256], F32), ("VB", [P, 2, 3, P], F32),
             ("QA", [P, 2, 256], F32), ("QbS", [P, 3, 4, P], F32), ("QaS", [P, P], F32),
             ("kca", [P, P], F32), ("vca", [P, P], F32), ("S", [P, 2, 768], F32), ("PT", [P, 2, 768], F32)],
            [("gt", [P, 4, 2, NTOK], F32), ("xres", [P, 2, 2, NTOK], F32), ("t1", [P, 2, NTOK], F32),
             ("t2", [P, 2, 2, NTOK], F32), ("lnrow", [P, 3, NTOK], F32)],
        )
        qTa, qTb = qT[:, 0:8], qT[:, 8:20]
        oT = sb("oT", [P, 12, NTOK])
        ident = sb("ident", [P, P])
        onesD = sb("onesD", [P, P])
        mask_p = sb("mask_p", [P, 3, 256])
        mask_c = sb("mask_c", [P, 4, P])
        mask_n = sb("mask_n", [P, 4, 120])
        sink_p = sb("sink_p", [P, QH_A])
        sink_s = sb("sink_s", [P, 2])
        vecs = sb("vecs", [P, 5 * 16 + 64])
        st = sb("st", [P, 2, 16])
        ln1g, ln1b, ln2g, ln2b, bff2 = (vecs[:, 16 * k:16 * k + 16] for k in range(5))
        bff1 = vecs[:, 80:144]

        psM = [ctx.enter_context(nc.psum_tensor(f"psM{k}", [P, 2, 512], F32)) for k in range(2)]
        psT = ctx.enter_context(nc.psum_tensor("psT", [P, 2, 512], F32))
        psO = ctx.enter_context(nc.psum_tensor("psO", [P, 2, 512], F32))
        psTf = psT[:, :, :].rearrange("p a b -> p (a b)")

        gates_d = nc.dram_tensor("gates_scratch", [32, P, NTOK], F32, kind="Internal").ap()
        kvn_d = nc.dram_tensor("kv_scratch", [NTOK, 2 * KVW], F32, kind="Internal").ap()


        loaded = [sem(f"loaded{k}") for k in range(RING)]
        hi_done, lo_done = sem("hi_done"), sem("lo_done")
        chunk_done = sem("chunk_done")
        evac = [sem("evac0"), sem("evac1")]
        const_in = sem("const_in")
        x_in = [sem(f"x_in{k}") for k in range(4)]
        x_hi, x_lo = sem("x_hi"), sem("x_lo")
        rot_ready, rope_a, rope_b = sem("rot_ready"), sem("rope_a"), sem("rope_b")
        kcopy, dup_ready = sem("kcopy"), sem("dup_ready")
        turned, turned_out = sem("turned"), sem("turned_out")
        kv_stored = [sem("kv_stored0"), sem("kv_stored1")]
        gate_stored = [sem("gate_stored0"), sem("gate_stored1")]
        out_kv, out_cache, y_out = sem("out_kv"), sem("out_cache"), sem("y_out")
        zeroed, staged = sem("zeroed"), sem("staged")
        kc_in, vc_in = sem("kc_in"), sem("vc_in")
        scores, masked, maxed, sinkmax, shifted = (sem(n) for n in ("scores", "masked", "maxed", "sinkmax", "shifted"))
        exped, denom, recip, normed = (sem(n) for n in ("exped", "denom", "recip", "normed"))
        pT, pT_out, pv, o_out = (sem(n) for n in ("pT", "pT_out", "pv", "o_out"))
        sums, sums_out = sem("sums"), sem("sums_out")
        o_hi, o_lo = sem("o_hi"), sem("o_lo")
        g_in = [sem(f"g_in{k}") for k in range(4)]
        m_sum, m_hi, m_lo = sem("m_sum"), sem("m_hi"), sem("m_lo")
        xr_in = [sem("xr_in0"), sem("xr_in1")]
        ln_dve, ln_pe, ln_act = sem("ln_dve"), sem("ln_pe"), sem("ln_act")
        h_hi, h_lo, r_init = sem("h_hi"), sem("h_lo"), sem("r_init")
        u_done, u_hi, u_lo = sem("u_done"), sem("u_hi"), sem("u_lo")

        G_QB, G_KVA, G_K, G_V, G_G, G_BR, G_WO, G_FF = 4, 10, 11, 17, 23, 39, 55, 63
        C_BR = 4 * G_BR
        C_WO = C_BR + 24
        C_FF = C_WO + 32
        G_BLK, C_BLK = 16, 64
        C_KVA, C_QB, C_K = QH_A * HD, QH_A * HD + 256, QH_A * HD + 256 + NG * 512
        C_GATE = C_K + 2 * NG * 512

        w_in, w_a, w_b, w_out = (a[n][0] for n in ("w_in", "w_branch_a", "w_branch_b", "w_out"))
        w1, w2 = a["w_ff1"][0], a["w_ff2"][0]

        def projections(eng, step):
            step(0, 0, 0, "q", None)
            step(1, 0, 1, "q", None)
            with eng.Fori(0, 4) as i:
                for c in range(2, 4):
                    step(i * 2 + c, i, c, "q", None)
            step(10, 0, 10, "kva", None)
            step(11, 0, 11, "k", "kva")
            with eng.Fori(0, 2) as i:
                for c in range(12, 14):
                    step(i * 2 + c, i, c, "k", "k")
            step(16, 0, 16, "k", "k")
            step(17, 0, 17, "v", "k")
            with eng.Fori(0, 2) as i:
                for c in range(18, 20):
                    step(i * 2 + c, i, c, "v", "v")
            step(22, 0, 22, "v", "v")
            step(23, 0, 23, "gate", "v")
            step(24, 0, 24, "gate", None)
            with eng.Fori(0, 7) as i:
                for c in range(25, 27):
                    step(i * 2 + c, i, c, "gate", None)

        UNITS = [("B", 0, 0), ("B", 0, 1), ("SB", 0, 0), ("SA", 0, 0), ("A", 0, 0), ("A", 0, 1),
                 ("B", 1, 0), ("B", 1, 1), ("SB", 1, 0), ("SA", 1, 0), ("A", 1, 0), ("A", 1, 1)]
        NU = len(UNITS)
        STAGED = {0: 1, 2: 2, 3: 3, 4: 4, 8: 5, 9: 6}
        NSTAGE = len(STAGED)

        def units(eng, body):
            def at(j, s):
                def one(d):
                    q, k = divmod(s + d, NU)
                    if isinstance(j, int):
                        number = j * NU + s + d
                        return (j + q, k, number) if 0 <= number < 4 * NU else None
                    return (j + q if q else j), k, j * NU + (s + d)
                return one
            for s in range(2):
                body(at(0, s))
            with eng.Fori(0, 3) as j:
                for s in range(2, NU + 2):
                    body(at(j, s))
            for s in range(2, NU):
                body(at(3, s))

        def wait(eng, s, value):
            if not (isinstance(value, int) and value <= 0):
                eng.wait_ge(s, value)

        block = ctx.enter_context(nc.Block())

        @block.sync
        def _(sp):
            def load(c, slot, w, row, col):
                if not (isinstance(c, int) and c < RING):
                    sp.wait_ge(lo_done, c - (RING - 1))
                src = w[bass.ds(row, KT * P), bass.ds(col, GW)].rearrange("(t p) n -> p t n", p=P)
                sp.dma_start(raw[:, slot], src).then_inc(loaded[slot], 16)

            def load_group(c, w, row, col):
                for j in range(4):
                    load(c + j, j, w, row + j * KT * P, col)

            xv = a["xT"].rearrange("(t p) n -> p t n", p=P)
            for j in range(4):
                sp.dma_start(xraw[:, 4 * j:4 * j + 4], xv[:, 4 * j:4 * j + 4]).then_inc(x_in[j], 16)
                load(j, j, w_in, j * KT * P, 0)
            for dst, name in ((rope, "rope"), (ident, "ident"), (mask_p, "mask_p"), (mask_c, "mask_c"),
                              (mask_n, "mask_n"), (sink_p, "sink_p"), (sink_s, "sink_s"), (vecs, "vecs")):
                sp.dma_start(dst[:], a[name]).then_inc(const_in, 16)
            with sp.Fori(0, 3) as i:
                load_group(i * 4 + 4, w_in, 0, i * GW + GW)
            with sp.Fori(0, 6) as i:
                load_group(i * 4 + 4 * G_QB, w_in, 0, i * GW + C_QB)
            load_group(4 * G_KVA, w_in, 0, C_KVA)
            with sp.Fori(0, 12) as i:
                load_group(i * 4 + 4 * G_K, w_in, 0, i * GW + C_K)
            with sp.Fori(0, 16) as i:
                load_group(i * 4 + 4 * G_G, w_in, 0, i * GW + C_GATE)
            with sp.Fori(0, 2) as i:
                for q in range(4):
                    for j in range(3):
                        load(i * 12 + (C_BR + 3 * q + j), (3 * q + j) % RING, w_b if j == 2 else w_a,
                             0 if j == 2 else j * KT * P, i * (4 * GW) + q * GW)
            with sp.Fori(0, 8) as i:
                load_group(i * 4 + C_WO, w_out, 0, i * GW)
            with sp.Fori(0, 4) as b:
                with sp.Fori(0, 8) as q:
                    load_group(b * C_BLK + q * 4 + C_FF, w1, 0, b * (8 * GW) + q * GW)
                with sp.Fori(0, 8) as q:
                    load_group(b * C_BLK + q * 4 + (C_FF + 32), w2, b * D, q * GW)

        @block.gpsimd
        def _(pool):
            nc.gpsimd.memset(onesD[:], 1.0 / D).then_inc(zeroed, 1)

            def kcopy_step(g, i, c, kind, turn):
                if kind == "k":
                    pool.wait_ge(evac[c % 2], i + (c // 2 + 1))
                    pool.tensor_copy(kTb[:, bass.ds((g - G_K) * 2, 2)], tT[:, c % 2]).then_inc(kcopy, 1)

            kcopy_step(11, 0, 11, "k", None)
            with pool.Fori(0, 2) as i:
                for c in range(12, 14):
                    kcopy_step(i * 2 + c, i, c, "k", None)
            kcopy_step(16, 0, 16, "k", None)

            pool.wait_ge(kv_stored[0], 16 * 14)
            pool.wait_ge(kv_stored[1], 16 * 14)
            kv_rows = kvn_d.rearrange("t (s c) -> t s c", s=2)
            for name, col, wid, win in (("a", 0, 128, 128), ("b1", 128, 512, 128), ("b2", 640, 512, 512), ("b3", 1152, 512, 2048)):
                rows = min(win, SEQ)
                dst = o[name + "_p"][0, 0].rearrange("t s h d -> t s (h d)")
                pool.dma_start(dst, kv_rows[SEQ - rows:SEQ, :, col:col + wid]).then_inc(out_kv, 16)
                keep = min(win, PAST + DT)
                for s in range(2):
                    dst = o[name + "_s"][0, :, keep - DT:keep, s].rearrange("n t h d -> n t (h d)")
                    src = kv_rows[SEQ:NTOK, s, col:col + wid].rearrange("(n t) c -> n t c", n=DB)
                    pool.dma_start(dst, src).then_inc(out_kv, 16)

            def load_k(n):
                pool.dma_start(kcache[:].rearrange("p a c k -> p (a c k)"),
                               a["kT_b"][bass.ds(n, 1)].rearrange("n p k -> (n p) k")).then_inc(kc_in, 16)
                pool.dma_start(kca[:], a["kT_a"][bass.ds(n, 1)].rearrange("n p k -> (n p) k")).then_inc(kc_in, 16)

            def load_v(n):
                pool.dma_start(vca[:], a["cache_a_kv"][0, bass.ds(n, 1), :, 1].rearrange("n r h d -> (n r) (h d)")).then_inc(vc_in, 16)
                pool.dma_start(vcache[:].rearrange("p c k -> p (c k)"),
                               a["v_b"][bass.ds(n, 1)].rearrange("n p k -> (n p) k")).then_inc(vc_in, 16)

            pool.wait_ge(chunk_done, C_BR)
            pool.wait_ge(turned_out, 13)
            pool.wait_ge(gate_stored[0], 16 * 8)
            pool.wait_ge(gate_stored[1], 16 * 8)
            load_k(0)
            load_v(0)
            with pool.Fori(0, 3) as i:
                for e in range(2):
                    pool.wait_ge(scores, i * NU + (4 + 6 * e))
                    pool.wait_ge(chunk_done, C_BR)
                    load_k(i * 2 + (1 + e))
                    pool.wait_ge(pv, i * NU + (5 + 6 * e))
                    pool.wait_ge(chunk_done, C_BR)
                    load_v(i * 2 + (1 + e))
            pool.wait_ge(scores, 3 * NU + 4)
            load_k(7)
            pool.wait_ge(pv, 3 * NU + 5)
            load_v(7)

            def load_gates(q, e):
                for k in range(2):
                    pool.dma_start(gt[:, 2 * e + k], gates_d[bass.ds(q * 2 + 16 * k, 2)].rearrange("t p n -> p t n")
                                   ).then_inc(g_in[2 * e + k], 16)

            pool.wait_ge(o_out, 4 * NU)
            pool.wait_ge(pv, 4 * NU)
            load_gates(0, 0)
            load_gates(1, 1)
            with pool.Fori(0, 3) as i:
                for e in range(2):
                    pool.wait_ge(m_sum, i * 2 + (1 + e))
                    pool.wait_ge(pv, 4 * NU)
                    load_gates(i * 2 + (2 + e), e)

            def load_x(q, e):
                pool.dma_start(xres[:, e], a["xT"][bass.ds(q * 256, 256)].rearrange("(t p) n -> p t n", p=P)
                               ).then_inc(xr_in[e], 16)

            load_x(0, 0)
            load_x(1, 1)
            with pool.Fori(0, 3) as i:
                pool.wait_ge(evac[1], i + ((G_WO + 1) // 2))
                pool.wait_ge(pv, 4 * NU)
                load_x(i * 2 + 2, 0)
                pool.wait_ge(evac[0], i + ((G_WO + 1) // 2 + 1))
                pool.wait_ge(pv, 4 * NU)
                load_x(i * 2 + 3, 1)

            with pool.Fori(0, DB) as n:
                piece = 0
                for name, win, parts in (("a", 128, 1), ("b1", 128, 1), ("b2", 512, 2), ("b3", 2048, 4)):
                    keep, past = min(win, PAST + DT), min(win, PAST)
                    cache = a[f"cache_{name}_kv"][0]
                    rows = (keep - DT) // parts
                    for q in range(parts):
                        pool.wait_ge(lo_done, n * 30 + (C_FF + 4 * piece))
                        pool.wait_ge(pv, 4 * NU)
                        dst = o[name + "_s"][0, bass.ds(n, 1), q * rows:(q + 1) * rows].rearrange("n t s h d -> (n t) (s h d)")
                        first = past - (keep - DT) + q * rows
                        src = cache[bass.ds(n, 1), first:first + rows].rearrange("n t s h d -> (n t) (s h d)")
                        pool.dma_start(dst, src).then_inc(out_cache, 16)
                        piece += 1
            pool.wait_ge(out_kv, 16 * 12)
            pool.wait_ge(out_cache, 16 * 8 * DB)
            pool.wait_ge(y_out, 16 * 4)

        @block.scalar
        def _(act):
            def split(q, slot, first=False):
                act.wait_ge(loaded[slot], q * 16 + 16)
                if not first:
                    act.wait_ge(chunk_done, q * 4 + (slot - RING + 1))
                act.activation(whi[:, slot], raw[:, slot], ACT.Copy).then_inc(hi_done, 1)

            for j in range(4):
                act.wait_ge(x_in[j], 16)
                act.activation(xhi[:, 4 * j:4 * j + 4], xraw[:, 4 * j:4 * j + 4], ACT.Copy).then_inc(x_hi, 1)
                split(0, j, first=True)

            def turn_out(g, i, c, kind):
                par = c % 2
                act.wait_ge(turned, g - 9)
                ps = psTf[:, 0:768].rearrange("p (c n) -> p c n", c=3)

                def move(dst, dcol, scol, n):
                    act.activation(dst[:, 0:2, dcol], ps[:, 0:2, scol:scol + n], ACT.Copy)
                    return act.activation(dst[0:64, 2, dcol], ps[0:64, 2, scol:scol + n], ACT.Copy)

                def store(src, scol, dcol, n, done=kv_stored[par]):
                    act.dma_start(kvn_d[0:256, bass.ds(dcol, n)].rearrange("(c p) n -> p c n", p=P),
                                  src[:, 0:2, scol]).then_inc(done, 16)
                    act.dma_start(kvn_d[256:NTOK, bass.ds(dcol, n)], src[0:64, 2, scol]).then_inc(done, 16)

                if kind == "kva":
                    move(kst[:, par], slice(0, P), 0, P)
                    move(vnat, slice(0, P), P, P).then_inc(turned_out, 1)
                    act.wait_ge(turned_out, 1)
                    store(kst[:, par], slice(0, P), 0, P)
                    store(vnat, slice(0, P), KVW, P, kv_stored[1])
                elif kind == "k":
                    act.wait_ge(kv_stored[par], i * 32 + {11: 32, 12: 32, 15: 96, 16: 96}[c])
                    move(kst[:, par], slice(0, GW), 0, GW).then_inc(turned_out, 1)
                    act.wait_ge(turned_out, g - 9)
                    store(kst[:, par], slice(0, GW), (g - G_K) * GW + P, GW)
                else:
                    col = bass.ds((g - G_V) * GW + P, GW)
                    move(vnat, col, 0, GW).then_inc(turned_out, 1)
                    act.wait_ge(turned_out, g - 9)
                    store(vnat, col, (g - G_V) * GW + (KVW + P), GW)

            def step(g, i, c, kind, turn):
                par, h = c % 2, i + c // 2
                for j in range(4):
                    split(g + 1, j)
                act.wait_ge(chunk_done, g * 4 + 4)
                ps = psM[par]
                if kind in ("q", "k", "kva"):
                    n = 1 if kind == "kva" else 2
                    if c > 0:
                        act.wait_ge(evac[1 - par], i + ((c - 1) // 2 + 1))
                    for q in range(4):
                        last = act.activation(rot[32 * q:32 * q + 32, 0:n], ps[32 * (q ^ 1):32 * (q ^ 1) + 32, 0:n, 0:NTOK],
                                              ACT.Copy)
                    if kind == "kva":
                        last = act.activation(tT[:, par, 1], ps[:, 1, 0:NTOK], ACT.Copy)
                    last.then_inc(rot_ready, 1)
                elif kind == "v":
                    act.wait_ge(turned, g - 11)
                    if c <= 18:
                        act.wait_ge(kcopy, 7 if c == 18 else 6)
                    act.activation(tT[:, par], ps[:, :, 0:NTOK], ACT.Copy).then_inc(evac[par], 1)
                else:
                    if c > 24:
                        act.wait_ge(gate_stored[par], i * 16 + 16)
                    act.activation(gstage[:, par], ps[:, :, 0:NTOK], ACT.Sigmoid).then_inc(evac[par], 1)
                    act.wait_ge(evac[par], h + 1)
                    act.dma_start(gates_d[bass.ds((g - G_G) * 2, 2)].rearrange("t p n -> p t n"), gstage[:, par]
                                  ).then_inc(gate_stored[par], 16)
                if turn:
                    turn_out(g - 1, i, c - 1, turn)

            projections(act, step)

            def exps(j, k, U):
                kind, e, qb = UNITS[k]
                par = k % 2
                s = st[:, par]
                act.wait_ge(shifted, U + 1)
                nh, n = {"A": (2, P * (qb + 1)), "B": (1, 384 * (qb + 1)), "SB": (1, 576), "SA": (1, 192)}[kind]
                for hh in range(nh):
                    act.activation(S[:, par, hh * n:hh * n + n], S[:, par, hh * n:hh * n + n], ACT.Exp,
                                   bias=s[:, 2 + hh:3 + hh], accum_out=s[:, 4 + hh:5 + hh])
                act.activation(s[:, 6:6 + nh], s[:, 12:12 + nh], ACT.Exp).then_inc(exped, 1)

            def turned_probs(j, k, U):
                kind, e, qb = UNITS[k]
                out = PT[:, k % 2]
                act.wait_ge(pT, U + 1)
                if kind in ("A", "B"):
                    n = (384 if kind == "B" else 256) * (qb + 1)
                    act.activation(out[:, 0:n], psTf[:, 0:n], ACT.Copy).then_inc(pT_out, 1)
                else:
                    n = 512 if kind == "SB" else P
                    act.activation(out[:, 0:n], psTf[:, 0:n], ACT.Copy)
                    act.activation(out[0:64, 512:640], psTf[0:64, 512:640], ACT.Copy).then_inc(pT_out, 1)

            def sums_evac(j, k, U):
                act.wait_ge(sums, j * 2 + (UNITS[k][1] + 1))
                act.activation(onat[:], psO[:, k % 2], ACT.Copy).then_inc(sums_out, 1)

            def o_evac(j, k, U):
                kind, e, qb = UNITS[k]
                ps = psO[:, k % 2]
                act.wait_ge(pv, U + 1)
                if kind in ("A", "B"):
                    part = slice(64 * e, 64 * e + 64) if kind == "B" else slice(0, P)
                    tile = j + (8 if kind == "B" else 4 * e)
                    last = act.activation(oT[part, bass.ds(tile, 1), P * qb:P * qb + P],
                                          ps[part, 0:P].rearrange("p (a n) -> p a n", a=1), ACT.Copy)
                elif kind == "SB":
                    for hh in range(2):
                        src = ps[64 * hh:64 * hh + 64, 0:64].rearrange("p (a c h e) -> p a h e c", a=4, c=4, h=2)[:, :, hh]
                        dst = oT[64 * hh:64 * hh + 64, 8:12, bass.ds(j * 16 + (SEQ + 8 * e), 8)].rearrange("p a (e c) -> p a e c", e=2)
                        last = act.activation(dst, src, ACT.Copy)
                else:
                    for kv in range(2):
                        for w in range(2):
                            src = ps[64 * kv:64 * kv + 64, 64 * kv:64 * kv + 64].rearrange("p (t w i) -> p t w i", t=4, w=2)[:, :, w]
                            dst = oT[64 * w:64 * w + 64, 4 * kv:4 * kv + 4, bass.ds(j * 16 + (SEQ + 8 * e), 8)]
                            last = act.activation(dst, src, ACT.Copy)
                last.then_inc(o_out, 1)

            exps(0, 0, 0)

            def attend(at):
                if at(1):
                    exps(*at(1))
                turned_probs(*at(0))
                if at(-2) and UNITS[at(-2)[1]][0] == "SB":
                    o_evac(*at(-2))
                if at(-1):
                    (sums_evac if UNITS[at(-1)[1]][0] == "SB" else o_evac)(*at(-1))

            units(act, attend)
            o_evac(3, NU - 1, 4 * NU - 1)

            act.wait_ge(o_out, 4 * NU)
            for j in range(3):
                act.activation(ohi[:, 4 * j:4 * j + 4], oT[:, 4 * j:4 * j + 4], ACT.Copy).then_inc(o_hi, 1)

            with act.Fori(0, 2) as i:
                for q in range(4):
                    for j in range(3):
                        s = 3 * q + j
                        split(i * 3 + (C_BR // 4 + 1 + s // 4), s % 4)
                    act.wait_ge(m_sum, i * 4 + (q + 1))
                    act.activation(mhi[:, bass.ds(i * 8 + 2 * q, 2)], t2[:, q % 2], ACT.Copy).then_inc(m_hi, 1)

            with act.Fori(0, 8) as i:
                for j in range(4):
                    split(i + (C_WO // 4 + 1), j)

            def layer_norm(li, gam, bet):
                for half in range(2):
                    act.wait_ge(ln_dve, 30 * li + 2 + half)
                    act.activation(gt[:, :, :].rearrange("p a b n -> p (a b) n"), r[:, 8 * half:8 * half + 8], ACT.Square
                                   ).then_inc(ln_act, 1)
                act.wait_ge(ln_dve, 30 * li + 6)
                act.activation(lnrow[:, 0], lnrow[:, 0], ACT.Sqrt).then_inc(ln_act, 1)
                for j in range(4):
                    act.wait_ge(ln_dve, 30 * li + 8 + j)
                    for t in range(4 * j, 4 * j + 4):
                        last = act.activation(r[:, t], r[:, t], ACT.Identity, bias=bet[:, t:t + 1], scale=gam[:, t:t + 1])
                    last.then_inc(ln_act, 1)
                    act.wait_ge(ln_act, 7 * li + 4 + j)
                    if li == 0:
                        act.activation(hhi[:, 4 * j:4 * j + 4], r[:, 4 * j:4 * j + 4], ACT.Copy).then_inc(h_hi, 1)
                    else:
                        act.dma_start(o["yT"].rearrange("(t p) n -> p t n", p=P)[:, 4 * j:4 * j + 4],
                                      r[:, 4 * j:4 * j + 4]).then_inc(y_out, 16)

            layer_norm(0, ln1g, ln1b)

            def up(b, q, c):
                par = 1 - c
                for j in range(4):
                    split(b * 16 + q * 2 + (C_FF // 4 + 1 + c), j)
                act.wait_ge(chunk_done, b * C_BLK + q * 8 + (C_FF + 4 * c + 4))
                for t in range(2):
                    last = act.activation(t2[:, c, t], psM[par][:, t, 0:NTOK], ACT.Relu,
                                          bias=bff1[:, bass.ds(b * 16 + q * 4 + (2 * c + t), 1)])
                last.then_inc(evac[par], 1)
                act.wait_ge(u_done, b * 8 + q * 2 + (c + 1))
                act.activation(uhi[:, bass.ds(q * 4 + 2 * c, 2)], t2[:, c], ACT.Copy).then_inc(u_hi, 1)

            with act.Fori(0, 3) as b:
                with act.Fori(0, 4) as q:
                    up(b, q, 0)
                    up(b, q, 1)
                with act.Fori(0, 8) as q:
                    for j in range(4):
                        split(b * 16 + q + (C_FF // 4 + 9), j)
            with act.Fori(0, 4) as q:
                up(3, q, 0)
                up(3, q, 1)
            with act.Fori(0, 7) as q:
                for j in range(4):
                    split(q + (3 * 16 + C_FF // 4 + 9), j)
            layer_norm(1, ln2g, ln2b)

        @block.vector
        def _(dve):
            def split(q, slot, first=False):
                dve.wait_ge(hi_done, q * 4 + (slot + 1))
                if not first:
                    dve.wait_ge(chunk_done, q * 4 + (slot - RING + 1))
                dve.tensor_tensor(wlo[:, slot], raw[:, slot], whi[:, slot].bitcast(F32), ALU.subtract).then_inc(lo_done, 1)

            for j in range(4):
                dve.wait_ge(x_hi, j + 1)
                dve.tensor_tensor(xlo[:, 4 * j:4 * j + 4], xraw[:, 4 * j:4 * j + 4],
                                  xhi[:, 4 * j:4 * j + 4].bitcast(F32), ALU.subtract).then_inc(x_lo, 1)
                split(0, j, first=True)
            dve.wait_ge(const_in, 16 * 8)

            def step(g, i, c, kind, turn):
                par, h = c % 2, i + c // 2
                for j in range(4):
                    split(g + 1, j)
                if kind in ("v", "gate"):
                    return
                n = 1 if kind == "kva" else 2
                dst = {"q": lambda: qT[:, bass.ds(g * 2, 2)],
                       "k": lambda: tT[:, par], "kva": lambda: tT[:, par, 0:1]}[kind]()
                cos, sin = (rope[:, k:k + 1].broadcast_to([P, n, NTOK]) for k in range(2))
                dve.wait_ge(chunk_done, g * 4 + 4)
                if kind == "k" and c > 11:
                    dve.wait_ge(turned, g - 11)
                    dve.wait_ge(kcopy, g - 11)
                dve.wait_ge(rot_ready, g + 1)
                dve.tensor_tensor(dst, psM[par][:, 0:n, 0:NTOK], cos, ALU.mult).then_inc(rope_a, 1)
                dve.tensor_tensor(rot[:, 0:n], rot[:, 0:n], sin, ALU.mult).then_inc(rope_b, 1)
                dve.wait_ge(rope_a, g + 1)
                dve.wait_ge(rope_b, g + 1)
                dve.tensor_tensor(dst, dst, rot[:, 0:n], ALU.add).then_inc(evac[par], 1)
                if kind == "kva":
                    dve.wait_ge(evac[par], h + 1)
                    src = tT[:, par, 0]
                    dve.tensor_copy(kTa[:, 0], src)
                    for kv in range(2):
                        for half in range(2):
                            last = dve.tensor_copy(kTa[64 * half:64 * half + 64, 1 + kv], src[64 * kv:64 * kv + 64])
                    last.then_inc(kcopy, 1)

            projections(dve, step)

            dve.wait_ge(turned_out, 13)
            dve.wait_ge(kcopy, 7)
            dve.wait_ge(kv_stored[0], 16 * 14)
            dve.wait_ge(kv_stored[1], 16 * 14)
            dve.wait_ge(gate_stored[0], 16 * 8)
            dve.wait_ge(gate_stored[1], 16 * 8)
            dve.memset(QbS[:], 0.0)
            dve.tensor_copy(vnat[64:P, 2, P:P + 512], vnat[0:64, 2, P + 512:P + 1024])
            dve.memset(QaS[:], 0.0).then_inc(zeroed, 1)
            dve.wait_ge(zeroed, 2)

            def stage(j, k, U):
                kind, e, qb = UNITS[k]
                if k == 0:
                    wait(dve, pv, U - 4)
                    q4, k4 = (t.rearrange("p (g a) n -> p g a n", g=3) for t in (qTb, kTb[:, :, :]))
                    dve.tensor_copy(QB[:], q4[:, :, bass.ds(j, 1), 0:256].rearrange("p g a n -> p g (a n)"))
                    dve.tensor_copy(KB[:], k4[:, :, bass.ds(j, 1), 0:256].rearrange("p g a n -> p g (a n)"))
                    for kb in range(2):
                        last = dve.tensor_copy(VB[:, kb], vnat[:, kb, P:KVW].rearrange("p (g n) -> p g n", g=3)[:, :, bass.ds(j * P, P)])
                elif k == 4:
                    q2 = qTa.rearrange("p (a b) n -> p a b n", a=2)
                    last = dve.tensor_copy(QA[:], q2[:, :, bass.ds(j, 1), 0:256].rearrange("p a b n -> p a (b n)"))
                elif kind == "SB":
                    for g in range(3):
                        for hh in range(2):
                            src = qTb[64 * hh:64 * hh + 64, 4 * g:4 * g + 4, bass.ds(j * 16 + (SEQ + 8 * e), 8)].rearrange("p a (e c) -> p a c e", e=2)
                            for pr in range(4):
                                dst = QbS[64 * hh:64 * hh + 64, g, pr].rearrange("p (c w) -> p c w", c=4)[:, :, 4 * pr + 2 * hh:4 * pr + 2 * hh + 2]
                                last = dve.tensor_copy(dst, src[:, pr])
                elif kind == "SA":
                    for kv in range(2):
                        for w in range(2):
                            dst = QaS[64 * kv:64 * kv + 64, 64 * kv:64 * kv + 64].rearrange("p (t w i) -> p t w i", t=4, w=2)[:, :, w]
                            src = qTa[64 * w:64 * w + 64, 4 * kv:4 * kv + 4, bass.ds(j * 16 + (SEQ + 8 * e), 8)]
                            last = dve.tensor_copy(dst, src)
                else:
                    return
                last.then_inc(staged, 1)

            def front(j, k, U):
                kind, e, qb = UNITS[k]
                par = k % 2
                ps = psM[par][:, :, :].rearrange("p a (b n) -> p (a b) n", b=2)
                s, Sp = st[:, par], S[:, par]
                nk = P * (qb + 1)
                pm = mask_p[:, :, 256 - nk:256]
                dve.wait_ge(scores, U + 1)
                wait(dve, pT, U - 1)
                if kind == "B":
                    nh, n = 1, 3 * nk
                    last = dve.scalar_tensor_tensor(Sp[:, 0:n].rearrange("p (g k) -> p g k", g=3), ps[:, 0:3, 0:nk], SCALE, pm,
                                                    ALU.mult, ALU.add)
                elif kind == "A":
                    nh, n = 2, nk
                    for hh in range(2):
                        last = dve.scalar_tensor_tensor(Sp[:, hh * nk:hh * nk + nk], ps[:, 2 * hh, 0:nk], SCALE, pm[:, 0], ALU.mult, ALU.add)
                else:
                    b0, nb = (0, 3) if kind == "SB" else (3, 1)
                    nh, n = 1, 192 * nb
                    cached, new = (Sp[:, P * nb * h:(P + 64 * h) * nb].rearrange("p (g k) -> p g k", g=nb) for h in range(2))
                    dve.scalar_tensor_tensor(cached, ps[:, 0:nb, 0:P], SCALE, mask_c[:, b0:b0 + nb], ALU.mult, ALU.add)
                    win = bass.ds(j * (-16) + (56 - 8 * e), 64)
                    last = dve.scalar_tensor_tensor(new, ps[:, 0:nb, P:192], SCALE, mask_n[:, b0:b0 + nb, win],
                                                    ALU.mult, ALU.add)
                last.then_inc(masked, 1)
                dve.wait_ge(masked, U + 1)
                dve.tensor_reduce(s[:, 0:nh], Sp[:, 0:nh * n].rearrange("p (h k) -> p h k", h=nh), AX.X, ALU.max).then_inc(maxed, 1)
                if kind == "A":
                    sink = sink_p[:, bass.ds(j * 2 + 8 * e, 2)]
                else:
                    sink = sink_s[:, 0:1] if kind == "SA" else sink_s[:, 1:2]
                dve.wait_ge(maxed, U + 1)
                dve.tensor_tensor(s[:, 0:nh], s[:, 0:nh], sink, ALU.max).then_inc(sinkmax, 1)
                dve.wait_ge(sinkmax, U + 1)
                dve.tensor_scalar(s[:, 2:2 + nh], s[:, 0:nh], -1.0, None, ALU.mult)
                dve.tensor_tensor(s[:, 12:12 + nh], sink, s[:, 0:nh], ALU.subtract).then_inc(shifted, 1)

            def back(j, k, U):
                kind, e, qb = UNITS[k]
                s, Sp = st[:, k % 2], S[:, k % 2]
                nh, n = {"A": (2, P * (qb + 1)), "B": (1, 384 * (qb + 1)), "SB": (1, 576), "SA": (1, 192)}[kind]
                dve.wait_ge(exped, U + 1)
                dve.tensor_tensor(s[:, 8:8 + nh], s[:, 4:4 + nh], s[:, 6:6 + nh], ALU.add).then_inc(denom, 1)
                dve.wait_ge(denom, U + 1)
                dve.reciprocal(s[:, 10:10 + nh], s[:, 8:8 + nh]).then_inc(recip, 1)
                dve.wait_ge(recip, U + 1)
                for hh in range(nh):
                    last = dve.tensor_scalar(Sp[:, hh * n:hh * n + n], Sp[:, hh * n:hh * n + n], s[:, 10 + hh:11 + hh], None, ALU.mult)
                last.then_inc(normed, 1)

            for k in range(3):
                stage(0, k, k)
            front(0, 0, 0)

            def attend(at):
                if at(3):
                    stage(*at(3))
                if at(1):
                    front(*at(1))
                back(*at(0))

            units(dve, attend)

            for j in range(3):
                dve.wait_ge(o_hi, j + 1)
                dve.tensor_tensor(olo[:, 4 * j:4 * j + 4], oT[:, 4 * j:4 * j + 4], ohi[:, 4 * j:4 * j + 4].bitcast(F32),
                                  ALU.subtract).then_inc(o_lo, 1)

            with dve.Fori(0, 2) as i:
                for q in range(4):
                    c0 = C_BR + 3 * q
                    for j in range(2):
                        s = 3 * q + j
                        split(i * 3 + (C_BR // 4 + 1 + s // 4), s % 4)
                    dve.wait_ge(chunk_done, i * 12 + (c0 + 2))
                    dve.wait_ge(g_in[2 * (q % 2)], i * 32 + 16 * (q // 2 + 1))
                    dve.tensor_tensor(t1[:], psM[1][:, :, 0:NTOK], gt[:, 2 * (q % 2)], ALU.mult).then_inc(evac[1], 1)
                    s = 3 * q + 2
                    split(i * 3 + (C_BR // 4 + 1 + s // 4), s % 4)
                    dve.wait_ge(chunk_done, i * 12 + (c0 + 3))
                    dve.wait_ge(g_in[2 * (q % 2) + 1], i * 32 + 16 * (q // 2 + 1))
                    dve.tensor_tensor(t2[:, q % 2], psM[0][:, :, 0:NTOK], gt[:, 2 * (q % 2) + 1], ALU.mult).then_inc(evac[0], 1)
                    dve.wait_ge(evac[1], i * 4 + (q + G_BR // 2 + 1))
                    dve.wait_ge(evac[0], i * 4 + (q + (G_BR + 1) // 2 + 1))
                    dve.tensor_tensor(t2[:, q % 2], t1[:], t2[:, q % 2], ALU.add).then_inc(m_sum, 1)
                    dve.wait_ge(m_hi, i * 4 + (q + 1))
                    dve.tensor_tensor(mlo[:, bass.ds(i * 8 + 2 * q, 2)], t2[:, q % 2], mhi[:, bass.ds(i * 8 + 2 * q, 2)].bitcast(F32),
                                      ALU.subtract).then_inc(m_lo, 1)

            with dve.Fori(0, 4) as i:
                for c in range(2):
                    for j in range(4):
                        split(i * 2 + (C_WO // 4 + 1 + c), j)
                    dve.wait_ge(chunk_done, i * 8 + (C_WO + 4 * c + 4))
                    dve.wait_ge(xr_in[c], i * 16 + 16)
                    dve.scalar_tensor_tensor(r[:, bass.ds(i * 4 + 2 * c, 2)], xres[:, c], ALPHA, psM[1 - c][:, :, 0:NTOK],
                                             ALU.mult, ALU.add).then_inc(evac[1 - c], 1)

            def layer_norm(li):
                base = 30 * li
                row = [lnrow[:, k] for k in range(3)]
                g8 = gt[:, :, :].rearrange("p a b n -> p n (a b)")
                dve.tensor_reduce(row[0], r[:, :, :].rearrange("p t n -> p n t"), AX.X, ALU.add).then_inc(ln_dve, 1)
                dve.wait_ge(ln_pe, 2 * li + 1)
                dve.tensor_tensor(r[:], r[:], psT[:, 0:1, 0:NTOK].broadcast_to([P, 16, NTOK]), ALU.subtract).then_inc(ln_dve, 1)
                dve.wait_ge(ln_act, 7 * li + 1)
                dve.tensor_reduce(row[1], g8, AX.X, ALU.add).then_inc(ln_dve, 1)
                dve.wait_ge(ln_act, 7 * li + 2)
                dve.tensor_reduce(row[2], g8, AX.X, ALU.add).then_inc(ln_dve, 1)
                dve.wait_ge(ln_dve, base + 4)
                dve.tensor_tensor(row[1], row[1], row[2], ALU.add).then_inc(ln_dve, 1)
                dve.wait_ge(ln_pe, 2 * li + 2)
                dve.tensor_scalar(row[0], psT[:, 1, 0:NTOK], EPS, None, ALU.add).then_inc(ln_dve, 1)
                dve.wait_ge(ln_act, 7 * li + 3)
                dve.reciprocal(row[1], row[0]).then_inc(ln_dve, 1)
                dve.wait_ge(ln_dve, base + 7)
                for j in range(4):
                    part = r[:, 4 * j:4 * j + 4]
                    dve.tensor_tensor(part, part, lnrow[:, 1:2].broadcast_to([P, 4, NTOK]), ALU.mult).then_inc(ln_dve, 1)

            dve.wait_ge(evac[1], G_FF // 2 + 0)
            dve.wait_ge(evac[0], G_FF // 2 + 1)
            layer_norm(0)
            for j in range(4):
                dve.wait_ge(h_hi, j + 1)
                dve.tensor_tensor(hlo[:, 4 * j:4 * j + 4], r[:, 4 * j:4 * j + 4], hhi[:, 4 * j:4 * j + 4].bitcast(F32),
                                  ALU.subtract).then_inc(h_lo, 1)
            dve.wait_ge(h_lo, 4)
            for t in range(16):
                last = dve.tensor_scalar(r[:, t], r[:, t], ALPHA, bff2[:, t:t + 1], ALU.mult, ALU.add)
            last.then_inc(ln_dve, 30 - 11)
            dve.wait_ge(ln_dve, 30)

            def up(b, q, c):
                for j in range(4):
                    split(b * 16 + q * 2 + (C_FF // 4 + 1 + c), j)
                dve.wait_ge(evac[1 - c], b * 8 + q + ((G_FF + c) // 2 + 1))
                dve.tensor_tensor(t2[:, c], t2[:, c], t2[:, c], ALU.mult).then_inc(u_done, 1)
                dve.wait_ge(u_hi, b * 8 + q * 2 + (c + 1))
                part = bass.ds(q * 4 + 2 * c, 2)
                dve.tensor_tensor(ulo[:, part], t2[:, c], uhi[:, part].bitcast(F32), ALU.subtract).then_inc(u_lo, 1)

            def down(b, q, c, last=False):
                if not last:
                    for j in range(4):
                        split(b * 16 + q * 2 + (C_FF // 4 + 9 + c), j)
                dve.wait_ge(chunk_done, b * C_BLK + q * 8 + (C_FF + 32 + 4 * c + 4))
                part = r[:, bass.ds(q * 4 + 2 * c, 2)]
                dve.tensor_tensor(part, part, psM[1 - c][:, :, 0:NTOK], ALU.add).then_inc(evac[1 - c], 1)

            with dve.Fori(0, 3) as b:
                with dve.Fori(0, 4) as q:
                    up(b, q, 0)
                    up(b, q, 1)
                with dve.Fori(0, 4) as q:
                    down(b, q, 0)
                    down(b, q, 1)
            with dve.Fori(0, 4) as q:
                up(3, q, 0)
                up(3, q, 1)
            with dve.Fori(0, 3) as q:
                down(3, q, 0)
                down(3, q, 1)
            down(3, 3, 0)
            down(3, 3, 1, last=True)
            dve.wait_ge(evac[1], (G_FF + 64) // 2)
            dve.wait_ge(evac[0], (G_FF + 65) // 2)
            layer_norm(1)

        @block.tensor
        def _(pe):
            def chunk(c, slot, ps, hi, lo, t0, first, last):
                pe.wait_ge(lo_done, c + 1)
                for k in range(KT):
                    for t in range(2):
                        wh, wl = (w[:, slot, k, P * t:P * t + P] for w in (whi, wlo))
                        out = ps[:, t, 0:NTOK]
                        pe.matmul(out, wh, hi[:, t0 + k], start=first and k == 0, stop=False)
                        pe.matmul(out, wh, lo[:, t0 + k], start=False, stop=False)
                        mm = pe.matmul(out, wl, hi[:, t0 + k], start=False, stop=last and k == KT - 1)
                mm.then_inc(chunk_done, 1)

            def group(c, ps, hi, lo, ready=None):
                for j in range(4):
                    if ready is not None:
                        pe.wait_ge(*ready(j))
                    chunk(c + j, j, ps, hi, lo, 4 * j, j == 0, j == 3)

            def turn(g, i, c):
                par = c % 2
                pe.wait_ge(evac[par], i + (c // 2 + 1))
                if c > 10:
                    pe.wait_ge(turned_out, g - 10)
                for k in range(3):
                    n = P if k < 2 else 64
                    for t in range(2):
                        mm = pe.transpose(psTf[0:n, k * GW + t * P:k * GW + t * P + P], tT[:, par, t, k * P:k * P + n], ident[:])
                mm.then_inc(turned, 1)

            def step(g, i, c, kind, turned_kind):
                par, h = c % 2, i + c // 2
                if c >= 2:
                    pe.wait_ge(evac[par], h)
                if c == 0:
                    group(g * 4, psM[par], xhi, xlo, ready=lambda j: (x_lo, j + 1))
                else:
                    group(g * 4, psM[par], xhi, xlo)
                if turned_kind:
                    if c == 11:
                        pe.wait_ge(const_in, 16 * 8)
                    turn(g - 1, i, c - 1)

            projections(pe, step)

            def unit_scores(j, k, U):
                kind, e, qb = UNITS[k]
                ps = psM[k % 2][:, :, :].rearrange("p a (b n) -> p (a b) n", b=2)
                if k in STAGED:
                    pe.wait_ge(staged, j * NSTAGE + STAGED[k])
                wait(pe, masked, U - 1)
                nk, qs = P * (qb + 1), slice(P * qb, P * qb + P)
                if kind == "B":
                    for g in range(3):
                        mm = pe.matmul(ps[:, g, 0:nk], QB[64 * e:64 * e + 64, g, qs], KB[64 * e:64 * e + 64, g, 0:nk],
                                       start=True, stop=True)
                elif kind == "A":
                    for hh in range(2):
                        mm = pe.matmul(ps[:, 2 * hh, 0:nk], QA[64 * hh:64 * hh + 64, e, qs], kTa[64 * hh:64 * hh + 64, 1 + e, 0:nk],
                                       start=True, stop=True)
                elif kind == "SB":
                    pe.wait_ge(kc_in, j * 64 + 32 * (e + 1))
                    for pr in range(4):
                        mm = pe.matmul(ps[:, 0, 0:P], QbS[:, 0, pr], kcache[:, pr, 0], start=pr == 0, stop=pr == 3)
                    for g in range(1, 3):
                        for pr in range(4):
                            for c in range(4):
                                mm = pe.matmul(ps[32 * c:32 * c + 32, g, 0:P], QbS[:, g, pr, 32 * c:32 * c + 32],
                                               kcache[:, pr, 1 + 4 * (g - 1) + c], start=pr == 0, stop=pr == 3)
                    for g in range(3):
                        for pr in range(4):
                            mm = pe.matmul(ps[:, g, P:192], QbS[:, g, pr], kTb[:, 4 * g + pr, SEQ:NTOK], start=pr == 0, stop=pr == 3)
                else:
                    pe.matmul(ps[:, 0, 0:P], QaS[:], kca[:], start=True, stop=True)
                    mm = pe.matmul(ps[:, 0, P:192], QaS[:], kTa[:, 0, SEQ:NTOK], start=True, stop=True)
                mm.then_inc(scores, 1)

            def turn_probs(j, k, U):
                kind, e, qb = UNITS[k]
                Sp = S[:, k % 2]
                pe.wait_ge(normed, U + 1)
                wait(pe, pT_out, U)
                if kind in ("A", "B"):
                    for t in range((3 if kind == "B" else 2) * (qb + 1)):
                        mm = pe.transpose(psTf[:, t * P:t * P + P], Sp[:, t * P:t * P + P], ident[:])
                else:
                    full = 4 if kind == "SB" else 1
                    for t in range(full):
                        pe.transpose(psTf[:, t * P:t * P + P], Sp[:, t * P:t * P + P], ident[:])
                    mm = pe.transpose(psTf[0:64, 512:640], Sp[:, full * P:full * P + 64], ident[:])
                mm.then_inc(pT, 1)

            def unit_values(j, k, U):
                kind, e, qb = UNITS[k]
                out, PTk, nb = psO[:, k % 2], PT[:, k % 2], 3 * (qb + 1)
                if kind in ("SB", "SA"):
                    pe.wait_ge(vc_in, j * 64 + 32 * (e + 1))
                pe.wait_ge(pT_out, U + 1)
                wait(pe, o_out, U - 1)
                if kind == "B":
                    for t in range(nb):
                        g, kb = divmod(t, qb + 1)
                        mm = pe.matmul(out[64 * e:64 * e + 64, 0:P], VB[:, kb, g, 64 * e:64 * e + 64], PTk[:, t * P:t * P + P],
                                       start=t == 0, stop=t == nb - 1)
                elif kind == "A":
                    for hh in range(2):
                        for kb in range(qb + 1):
                            t = hh * (qb + 1) + kb
                            mm = pe.matmul(out[64 * hh:64 * hh + 64, 0:P], vnat[:, kb, 64 * e:64 * e + 64], PTk[:, t * P:t * P + P],
                                           start=kb == 0, stop=kb == qb)
                elif kind == "SB":
                    pe.matmul(out, PTk[:, 0:P], vcache[:, 0], start=True, stop=False, skip_group_check=True)
                    for g in range(1, 3):
                        for c in range(4):
                            pe.matmul(out[32 * c:32 * c + 32], PTk[:, P * g + 32 * c:P * g + 32 * c + 32], vcache[:, 4 * g - 3 + c],
                                      start=False, stop=False, skip_group_check=True)
                    pe.matmul(out, PTk[:, 384:512], vnat[:, 2, P:P + 512], start=False, stop=False, skip_group_check=True)
                    pe.matmul(out, PTk[0:64, 512:640], vnat[0:64, 2, P + 1024:P + 1536], start=False, stop=True,
                              skip_group_check=True).then_inc(sums, 1)
                    return
                else:
                    pe.matmul(out[:, 0:P], vca[:], PTk[:, 0:P], start=True, stop=False)
                    mm = pe.matmul(out[:, 0:P], vnat[0:64, 2, 0:P], PTk[0:64, 512:640], start=False, stop=True)
                mm.then_inc(pv, 1)

            def turn_sums(j, k, U):
                pe.wait_ge(sums_out, j * 2 + (UNITS[k][1] + 1))
                rows = ident[:, :].rearrange("p (c w) -> p c w", c=4)
                for pr in range(4):
                    mm = pe.matmul(psO[:, k % 2, 16 * pr:16 * pr + 16].rearrange("p (c w) -> p c w", c=4),
                                   onat[:, P * pr:P * pr + P], rows[:, :, 4 * pr:4 * pr + 4], start=True, stop=True)
                mm.then_inc(pv, 1)

            pe.wait_ge(evac[0], G_BR // 2 + 1)
            pe.wait_ge(evac[1], G_BR // 2)
            unit_scores(0, 0, 0)
            unit_scores(0, 1, 1)

            def attend(at):
                if at(2):
                    unit_scores(*at(2))
                turn_probs(*at(0))
                if at(-2) and UNITS[at(-2)[1]][0] == "SB":
                    turn_sums(*at(-2))
                if at(-1):
                    unit_values(*at(-1))

            units(pe, attend)
            unit_values(3, NU - 1, 4 * NU - 1)

            with pe.Fori(0, 2) as i:
                for q in range(4):
                    s = 3 * q
                    pe.wait_ge(evac[1], i * 4 + (q + G_BR // 2))
                    for j in range(2):
                        pe.wait_ge(o_lo, j + 1)
                        chunk(i * 12 + (C_BR + s + j), (s + j) % 4, psM[1], ohi, olo, 4 * j, j == 0, j == 1)
                    pe.wait_ge(evac[0], i * 4 + (q + G_BR // 2 + 1))
                    pe.wait_ge(o_lo, 3)
                    chunk(i * 12 + (C_BR + s + 2), (s + 2) % 4, psM[0], ohi, olo, 8, True, True)

            with pe.Fori(0, 4) as i:
                for c in range(2):
                    pe.wait_ge(evac[1 - c], i + ((G_WO + c) // 2))
                    group(i * 8 + (C_WO + 4 * c), psM[1 - c], mhi, mlo, ready=lambda j: (m_lo, 2 * j + 2))

            def layer_norm(li):
                pe.wait_ge(ln_dve, 30 * li + 1)
                pe.matmul(psT[:, 0, 0:NTOK], onesD[:], lnrow[:, 0], start=True, stop=True).then_inc(ln_pe, 1)
                pe.wait_ge(ln_dve, 30 * li + 5)
                pe.matmul(psT[:, 1, 0:NTOK], onesD[:], lnrow[:, 1], start=True, stop=True).then_inc(ln_pe, 1)

            layer_norm(0)

            with pe.Fori(0, 4) as b:
                with pe.Fori(0, 4) as q:
                    for c in range(2):
                        pe.wait_ge(evac[1 - c], b * 8 + q + ((G_FF + c) // 2))
                        group(b * C_BLK + q * 8 + (C_FF + 4 * c), psM[1 - c], hhi, hlo, ready=lambda j: (h_lo, j + 1))
                with pe.Fori(0, 4) as q:
                    for c in range(2):
                        pe.wait_ge(evac[1 - c], b * 8 + q + ((G_FF + 8 + c) // 2))
                        group(b * C_BLK + q * 8 + (C_FF + 32 + 4 * c), psM[1 - c], uhi, ulo,
                              ready=lambda j: (u_lo, b * 8 + (2 * j + 2)))
            layer_norm(1)


_CACHES = ["cache_a_kv", "cache_b1_kv", "cache_b2_kv", "cache_b3_kv"]
_WEIGHTS = ["w_in", "w_branch_a", "w_branch_b", "w_out", "w_ff1", "w_ff2"]
_OUTS = {
    "yT": (D, NTOK),
    "a_p": (1, 1, 128, 2, 2, HD), "a_s": (1, DB, 128, 2, 2, HD),
    "b1_p": (1, 1, 128, 2, 8, HD), "b1_s": (1, DB, 128, 2, 8, HD),
    "b2_p": (1, 1, 256, 2, 8, HD), "b2_s": (1, DB, 512, 2, 8, HD),
    "b3_p": (1, 1, 256, 2, 8, HD), "b3_s": (1, DB, 1032, 2, 8, HD),
}


def constants():
    half = HD // 2
    inv = (1.0 / (np.float32(THETA) ** (np.arange(half, dtype=np.float32) / np.float32(half)))).astype(np.float32)
    pos = np.concatenate([np.arange(SEQ), np.tile(PAST + np.arange(DT), DB)]).astype(np.float32)
    ang = (pos[None, :] * inv[:, None]).astype(np.float32)
    cos, sin = np.cos(ang.astype(np.float64)), np.sin(ang.astype(np.float64))
    rope = np.stack([np.tile(cos, (4, 1)), np.tile(np.concatenate([-sin, sin]), (2, 1))], 1).astype(np.float32)

    mask_p = np.full((P, NG, 256), NEG, np.float32)
    q, s = np.arange(P)[:, None], np.arange(256)[None, :]
    for g, dil in enumerate(DIL):
        dist = P + q - s
        mask_p[:, g] = np.where((dist >= 0) & (dist % dil == 0) & (dist < 128 * dil), 0, NEG)

    mask_c = np.full((P, 4, P), NEG, np.float32)
    mask_n = np.full((P, 4, 120), NEG, np.float32)
    key = np.arange(P)
    for row in range(P):
        c, w = divmod(row, 32)
        if w < 16:
            i = c + 4 * (w % 2)
            mask_c[row, 0] = np.where(P + i - key < 128, 0, NEG)
            mask_c[row, 1] = np.where(512 + i - (4 * key + c) < 512, 0, NEG)
            mask_c[row, 2] = np.where(4 * (key % 2) + c == i, 0, NEG)
            for g, dil in enumerate(DIL):
                for t in range(DT):
                    if t <= i and (i - t) % dil == 0:
                        mask_n[row, g, 56 + t] = 0
        i = row % 8
        mask_c[row, 3] = np.where(P + i - key < 128, 0, NEG)
        mask_n[row, 3, 56:57 + i] = 0
    return {"rope": rope, "ident": np.eye(P, dtype=np.float32), "mask_p": mask_p, "mask_c": mask_c, "mask_n": mask_n}


def layouts(inputs):
    c = np.ascontiguousarray
    tiles = lambda v: v.reshape(-1, P).T
    x = np.concatenate([inputs["x_prompt"].reshape(SEQ, D), inputs["x_sample"].reshape(DB * DT, D)])
    ka, k1, k2, k3 = (inputs[n][0, :, :, 0] for n in _CACHES)
    va, v1, v2, v3 = (inputs[n][0, :, :, 1] for n in _CACHES)

    def chunks(t1, t2, t3):
        t3 = t3.reshape(DB, 64, 4, 4, H_B, HD)[:, :, 0:2].reshape(DB, P, 4, H_B, HD)
        return np.concatenate([t1[:, :, None], t2.reshape(DB, P, 4, H_B, HD), t3], 2)

    kT_b = chunks(k1, k2, k3).reshape(DB, P, CK, 4, P).transpose(0, 4, 3, 2, 1)
    sinks = inputs["a_sinks"].reshape(QH_A)
    sink_s = np.stack([np.repeat(sinks, DT), np.full(P, NEG, np.float32)], 1)
    out = {
        "xT": c(x.T), "kT_b": c(kT_b).reshape(DB, P, 4 * CK * P), "v_b": chunks(v1, v2, v3).reshape(DB, P, CK * 512),
        "kT_a": c(ka.reshape(DB, P, P).transpose(0, 2, 1)),
        "sink_p": c(np.broadcast_to(sinks, (P, QH_A))), "sink_s": c(sink_s),
        "vecs": c(np.concatenate([tiles(inputs[n][0]) for n in ("ln1_g", "ln1_b", "ln2_g", "ln2_b", "b_ff2", "b_ff1")], 1)),
    }
    out.update({n: c(inputs[n]) for n in _CACHES + _WEIGHTS})
    return out


def kernel(**inputs):
    import concourse.bacc as _bacc
    from concourse.bass_utils import run_bass_kernel_spmd as _run

    inputs = {n: np.asarray(v) for n, v in inputs.items()}
    nc = _bacc.Bacc("TRN2", target_bir_lowering=False, num_devices=1)
    arrays, ins, outs = {}, {}, {}
    for name, v in {**layouts(inputs), **constants()}.items():
        arrays[f"in_{name}_dram"] = v
        ins[name] = nc.dram_tensor(f"in_{name}_dram", v.shape, mybir.dt.from_np(v.dtype), kind="ExternalInput").ap()
    for name, shape in _OUTS.items():
        outs[name] = nc.dram_tensor(f"out_{name}_dram", shape, F32, kind="ExternalOutput").ap()
    program(nc, ins, outs)
    got = _run(nc, [arrays], core_ids=[0]).results[0]
    g = {name: got[f"out_{name}_dram"] for name in _OUTS}
    y = np.ascontiguousarray(g["yT"].T)
    return (y[:SEQ].reshape(1, SEQ, D), y[SEQ:].reshape(DB, DT, D), g["a_p"], g["a_s"], g["b1_p"], g["b1_s"],
            g["b2_p"], g["b2_s"], g["b3_p"], g["b3_s"])
```

```python
from contextlib import ExitStack

import concourse.bass as bass
import numpy as np
from concourse import mybir

F32 = mybir.dt.float32
F32R = mybir.dt.float32r
ACT = mybir.ActivationFunctionType
ALU = mybir.AluOpType
AX = mybir.AxisListType

P = 128
D = 2048
SEQ, DB, DT, PAST = 256, 8, 8, 1024
NTOK = SEQ + DB * DT
HD = 64
QH_A, H_B, NG = 16, 8, 3
GW = 256
KT = 4
RING = 4
NEG = -1e30
SCALE = HD ** -0.5
ALPHA = 2.0 ** 0.25
EPS = 1e-5
THETA = 10000.0
DIL = (1, 4, 16)
KVW = 1664
CK = 9
KN = P + DT


def program(nc, a, o):
    ctx = ExitStack()
    with ctx:
        def sb(name, shape, dt=F32):
            return ctx.enter_context(nc.sbuf_tensor("s_" + name, shape, dt))

        def sem(name):
            return ctx.enter_context(nc.semaphore(name))

        raw = sb("raw", [P, RING, KT, GW])
        whi = sb("whi", [P, RING, KT, GW], F32R)
        wlo = sb("wlo", [P, RING, KT, GW], F32R)

        def overlay(*sets):
            made, base = [], []
            for k, tensors in enumerate(sets):
                with ExitStack() as own:
                    made.append([own.enter_context(nc.sbuf_tensor("s_" + n, s, d)) for n, s, d in tensors])
            size = [sum(int(np.prod(s[1:])) for _, s, _ in t) for t in sets]
            ctx.enter_context(nc.sbuf_tensor(f"hold_{len(made)}_{sets[0][0][0]}", [P, max(size)], F32))
            return made

        (xhi, xlo), (kcache, vcache, vnewb, kca), (ohi, olo), (hhi, hlo) = overlay(
            [("xhi", [P, 16, NTOK], F32R), ("xlo", [P, 16, NTOK], F32R)],
            [("kcache", [P, 4, CK, KN], F32), ("vcache", [P, CK, 512], F32),
             ("vnewb", [NG * DT, 512], F32), ("kca", [P, KN], F32)],
            [("ohi", [P, 12, NTOK], F32R), ("olo", [P, 12, NTOK], F32R)],
            [("hhi", [P, 16, NTOK], F32R), ("hlo", [P, 16, NTOK], F32R)],
        )
        (xraw,), (vnat, qT, kTb, kTa), (r, mhi, mlo), (_, uhi, ulo) = overlay(
            [("xraw", [P, 16, NTOK], F32)],
            [("vnat", [P, 3, KVW], F32), ("qT", [P, 20, NTOK], F32),
             ("kTb", [P, 12, NTOK], F32), ("kTa", [P, 3, NTOK], F32)],
            [("r", [P, 16, NTOK], F32), ("mhi", [P, 16, NTOK], F32R), ("mlo", [P, 16, NTOK], F32R)],
            [("r_again", [P, 16, NTOK], F32), ("uhi", [P, 16, NTOK], F32R), ("ulo", [P, 16, NTOK], F32R)],
        )
        (tT, rot, kst, rope, gstage), (QB, KB, VB, QA, S, PT, QbS, QaS), (gt, xres, t1, t2, lnrow) = overlay(
            [("tT", [P, 2, 2, NTOK], F32), ("rot", [P, 2, NTOK], F32), ("kst", [P, 2, 3, GW], F32),
             ("rope", [P, 2, NTOK], F32), ("gstage", [P, 2, 2, NTOK], F32)],
            [("QB", [P, 3, 256], F32), ("KB", [P, 3, 256], F32), ("VB", [P, 2, 3, P], F32),
             ("QA", [P, 2, 256], F32), ("S", [P, 3, 768], F32), ("PT", [P, 2, 768], F32),
             ("QbS", [P, 3 * 512 + 32], F32), ("QaS", [P, P], F32)],
            [("gt", [P, 4, 2, NTOK], F32), ("xres", [P, 2, 2, NTOK], F32), ("t1", [P, 2, NTOK], F32),
             ("t2", [P, 2, 2, NTOK], F32), ("lnrow", [P, 3, NTOK], F32)],
        )
        squares = [t.rearrange("p a b n -> p (a b) n") for t in (gt[:, 0:2], gt[:, 2:4], xres[:, :, :], t2[:, :, :])]
        Qb = QbS[:, 0:3 * 512].rearrange("p (g a w) -> p g a w", g=3, a=4)
        qTa, qTb = qT[:, 0:8], qT[:, 8:20]
        oT = sb("oT", [P, 12, NTOK])
        vca = sb("vca", [P, P])
        vnewa = sb("vnewa", [DT, P])
        ident = sb("ident", [P, P])
        onesD = sb("onesD", [P, P])
        mask_p = sb("mask_p", [P, 3, 256])
        mask_c = sb("mask_c", [P, 4, P])
        mask_n = sb("mask_n", [P, 4, DT])
        sink_p = sb("sink_p", [P, QH_A])
        sink_s = sb("sink_s", [P, 1])
        vecs = sb("vecs", [P, 5 * 16 + 64])
        eps = sb("eps", [P, 2])
        st = sb("st", [P, 3, 16])
        ln1g, ln1b, ln2g, ln2b, bff2 = (vecs[:, 16 * k:16 * k + 16] for k in range(5))
        bff1 = vecs[:, 80:144]

        psM = [ctx.enter_context(nc.psum_tensor(f"psM{k}", [P, 2, 512], F32)) for k in range(2)]
        psT = ctx.enter_context(nc.psum_tensor("psT", [P, 2, 512], F32))
        psO = ctx.enter_context(nc.psum_tensor("psO", [P, 2, 512], F32))
        psTf = psT[:, :, :].rearrange("p a b -> p (a b)")

        gates_d = nc.dram_tensor("gates_scratch", [32, P, NTOK], F32, kind="Internal").ap()
        kvn_d = nc.dram_tensor("kv_scratch", [NTOK, 2 * KVW], F32, kind="Internal").ap()


        loaded = [sem(f"loaded{k}") for k in range(RING)]
        hi_done, lo_done = sem("hi_done"), sem("lo_done")
        chunk_done = sem("chunk_done")
        evac = [sem("evac0"), sem("evac1")]
        const_in = sem("const_in")
        x_in = [sem(f"x_in{k}") for k in range(4)]
        x_hi, x_lo = sem("x_hi"), sem("x_lo")
        rot_ready, rope_a, rope_b = sem("rot_ready"), sem("rope_a"), sem("rope_b")
        kcopy = sem("kcopy")
        turned, turned_out = sem("turned"), sem("turned_out")
        kv_stored = [sem("kv_stored0"), sem("kv_stored1")]
        gate_stored = [sem("gate_stored0"), sem("gate_stored1")]
        out_kv, out_cache, y_out = sem("out_kv"), sem("out_cache"), sem("y_out")
        zeroed, staged = sem("zeroed"), sem("staged")
        kc_in, vc_in = sem("kc_in"), sem("vc_in")
        keys_in = sem("keys_in")
        scores, masked, maxed, sinkmax, shifted = (sem(n) for n in ("scores", "masked", "maxed", "sinkmax", "shifted"))
        exped, denom, recip, normed = (sem(n) for n in ("exped", "denom", "recip", "normed"))
        pT, pT_out, pv, o_out = (sem(n) for n in ("pT", "pT_out", "pv", "o_out"))
        sums, sums_out = sem("sums"), sem("sums_out")
        o_hi, o_lo = sem("o_hi"), sem("o_lo")
        g_in = [sem(f"g_in{k}") for k in range(4)]
        m_sum, m_hi, m_lo = sem("m_sum"), sem("m_hi"), sem("m_lo")
        xr_in = [sem("xr_in0"), sem("xr_in1")]
        summed, mean_ready, centred, squared = (sem(n) for n in ("summed", "mean_ready", "centred", "squared"))
        paired, added = sem("paired"), sem("added")
        var_ready, rooted, rstd, scaled = (sem(n) for n in ("var_ready", "rooted", "rstd", "scaled"))
        affine_a, affine_d = sem("affine_a"), sem("affine_d")
        h_hi, h_lo, r_init = sem("h_hi"), sem("h_lo"), sem("r_init")
        u_done, u_hi, u_lo = sem("u_done"), sem("u_hi"), sem("u_lo")

        G_QB, G_KVA, G_K, G_V, G_G, G_BR, G_WO, G_FF = 4, 10, 11, 17, 23, 39, 55, 63
        C_BR = 4 * G_BR
        C_WO = C_BR + 24
        C_FF = C_WO + 32
        C_BLK = 64
        C_KVA, C_QB, C_K = QH_A * HD, QH_A * HD + 256, QH_A * HD + 256 + NG * 512
        C_GATE = C_K + 2 * NG * 512

        w_in, w_a, w_b, w_out = (a[n][0] for n in ("w_in", "w_branch_a", "w_branch_b", "w_out"))
        w1, w2 = a["w_ff1"][0], a["w_ff2"][0]

        def projections(eng, step):
            step(0, 0, 0, "q", None)
            step(1, 0, 1, "q", None)
            with eng.Fori(0, 4) as i:
                for c in range(2, 4):
                    step(i * 2 + c, i, c, "q", None)
            step(10, 0, 10, "kva", None)
            step(11, 0, 11, "k", "kva")
            with eng.Fori(0, 2) as i:
                for c in range(12, 14):
                    step(i * 2 + c, i, c, "k", "k")
            step(16, 0, 16, "k", "k")
            step(17, 0, 17, "v", "k")
            with eng.Fori(0, 2) as i:
                for c in range(18, 20):
                    step(i * 2 + c, i, c, "v", "v")
            step(22, 0, 22, "v", "v")
            step(23, 0, 23, "gate", "v")
            step(24, 0, 24, "gate", None)
            with eng.Fori(0, 7) as i:
                for c in range(25, 27):
                    step(i * 2 + c, i, c, "gate", None)

        UNITS = [("B", 0, 0), ("B", 0, 1), ("A", 0, 0), ("A", 0, 1), ("SB", 0, 0), ("SA", 0, 0),
                 ("B", 1, 0), ("B", 1, 1), ("A", 1, 0), ("A", 1, 1), ("SB", 1, 0), ("SA", 1, 0)]
        NU = len(UNITS)
        STAGED = {0: 1, 2: 2, 4: 3, 5: 4, 10: 5, 11: 6}
        NSTAGE = len(STAGED)
        SINKED = {2: 1, 3: 2, 5: 3, 8: 4, 9: 5, 11: 6}
        NSINK = len(SINKED)
        PEEL = 2

        def units(eng, body):
            def at(j, s):
                def one(d):
                    q, k = divmod(s + d, NU)
                    if isinstance(j, int):
                        number = j * NU + s + d
                        return (j + q, k, number) if 0 <= number < 4 * NU else None
                    return (j + q if q else j), k, j * NU + (s + d)
                return one
            for s in range(PEEL):
                body(at(0, s))
            with eng.Fori(0, 3) as j:
                for s in range(PEEL, NU + PEEL):
                    body(at(j, s))
            for s in range(PEEL, NU):
                body(at(3, s))

        def wait(eng, s, value):
            if not (isinstance(value, int) and value <= 0):
                eng.wait_ge(s, value)

        block = ctx.enter_context(nc.Block())

        @block.sync
        def _(sp):
            def load(c, slot, w, row, col):
                if not (isinstance(c, int) and c < RING):
                    sp.wait_ge(lo_done, c - (RING - 1))
                src = w[bass.ds(row, KT * P), bass.ds(col, GW)].rearrange("(t p) n -> p t n", p=P)
                sp.dma_start(raw[:, slot], src).then_inc(loaded[slot], 16)

            def load_group(c, w, row, col):
                for j in range(4):
                    load(c + j, j, w, row + j * KT * P, col)

            xv = a["xT"].rearrange("(t p) n -> p t n", p=P)
            for j in range(4):
                load(j, j, w_in, j * KT * P, 0)
                sp.dma_start(xraw[:, 4 * j:4 * j + 4], xv[:, 4 * j:4 * j + 4]).then_inc(x_in[j], 16)
            for dst, name in ((rope, "rope"), (ident, "ident"), (mask_p, "mask_p"), (mask_c, "mask_c"),
                              (mask_n, "mask_n"), (sink_p, "sink_p"), (sink_s, "sink_s"), (vecs, "vecs")):
                sp.dma_start(dst[:], a[name]).then_inc(const_in, 16)
            with sp.Fori(0, 3) as i:
                load_group(i * 4 + 4, w_in, 0, i * GW + GW)
            with sp.Fori(0, 6) as i:
                load_group(i * 4 + 4 * G_QB, w_in, 0, i * GW + C_QB)
            load_group(4 * G_KVA, w_in, 0, C_KVA)
            with sp.Fori(0, 12) as i:
                load_group(i * 4 + 4 * G_K, w_in, 0, i * GW + C_K)
            with sp.Fori(0, 16) as i:
                load_group(i * 4 + 4 * G_G, w_in, 0, i * GW + C_GATE)
            with sp.Fori(0, 2) as i:
                for q in range(4):
                    for j in range(3):
                        load(i * 12 + (C_BR + 3 * q + j), (3 * q + j) % RING, w_b if j == 2 else w_a,
                             0 if j == 2 else j * KT * P, i * (4 * GW) + q * GW)
            with sp.Fori(0, 8) as i:
                load_group(i * 4 + C_WO, w_out, 0, i * GW)
            with sp.Fori(0, 4) as b:
                with sp.Fori(0, 8) as q:
                    load_group(b * C_BLK + q * 4 + C_FF, w1, 0, b * (8 * GW) + q * GW)
                with sp.Fori(0, 8) as q:
                    load_group(b * C_BLK + q * 4 + (C_FF + 32), w2, b * D, q * GW)

        @block.gpsimd
        def _(pool):
            nc.gpsimd.memset(eps[:], EPS)
            nc.gpsimd.memset(onesD[:], 1.0 / D).then_inc(zeroed, 1)

            def kcopy_step(g, i, c, kind, turn):
                if kind == "k":
                    pool.wait_ge(evac[c % 2], i + (c // 2 + 1))
                    pool.tensor_copy(kTb[:, bass.ds((g - G_K) * 2, 2)], tT[:, c % 2]).then_inc(kcopy, 1)

            kcopy_step(11, 0, 11, "k", None)
            with pool.Fori(0, 2) as i:
                for c in range(12, 14):
                    kcopy_step(i * 2 + c, i, c, "k", None)
            kcopy_step(16, 0, 16, "k", None)

            pool.wait_ge(kv_stored[0], 16 * 14)
            pool.wait_ge(kv_stored[1], 16 * 14)
            kv_rows = kvn_d.rearrange("t (s c) -> t s c", s=2)
            for name, col, wid, win in (("a", 0, 128, 128), ("b1", 128, 512, 128), ("b2", 640, 512, 512), ("b3", 1152, 512, 2048)):
                rows = min(win, SEQ)
                dst = o[name + "_p"][0, 0].rearrange("t s h d -> t s (h d)")
                pool.dma_start(dst, kv_rows[SEQ - rows:SEQ, :, col:col + wid]).then_inc(out_kv, 16)
                keep = min(win, PAST + DT)
                for s in range(2):
                    dst = o[name + "_s"][0, :, keep - DT:keep, s].rearrange("n t h d -> n t (h d)")
                    src = kv_rows[SEQ:NTOK, s, col:col + wid].rearrange("(n t) c -> n t c", n=DB)
                    pool.dma_start(dst, src).then_inc(out_kv, 16)

            def load_k(n):
                pool.dma_start(kcache[:].rearrange("p a c k -> p (a c k)"),
                               a["kT_b"][bass.ds(n, 1)].rearrange("n p k -> (n p) k")).then_inc(kc_in, 16)
                pool.dma_start(kca[:], a["kT_a"][bass.ds(n, 1)].rearrange("n p k -> (n p) k")).then_inc(kc_in, 16)

            def load_v(n):
                pool.dma_start(vca[:], a["cache_a_kv"][0, bass.ds(n, 1), :, 1].rearrange("n r h d -> (n r) (h d)")).then_inc(vc_in, 16)
                pool.dma_start(vcache[:].rearrange("p c k -> p (c k)"),
                               a["v_b"][bass.ds(n, 1)].rearrange("n p k -> (n p) k")).then_inc(vc_in, 16)
                new = kvn_d[bass.ds(n * DT + SEQ, DT)]
                pool.dma_start(vnewa[:], new[:, KVW:KVW + P]).then_inc(vc_in, 16)
                for g in range(NG):
                    col = KVW + P + 512 * g
                    pool.dma_start(vnewb[DT * g:DT * g + DT], new[:, col:col + 512]).then_inc(vc_in, 16)

            def add_new_keys(n):
                pool.wait_ge(kc_in, n * 32 + 32)
                tok = bass.ds(n * DT + SEQ, DT)
                pool.tensor_copy(kca[:, P:KN], kTa[:, 0, tok])
                pool.tensor_copy(kcache[:, :, 0, P:KN], kTb[:, 0:4, tok])
                for g in range(1, NG):
                    src = kTb[:, 4 * g:4 * g + 4, tok].rearrange("p a (c n) -> p a c n", c=1).broadcast_to([P, 4, 4, DT])
                    last = pool.tensor_copy(kcache[:, :, 4 * g - 3:4 * g + 1, P:KN], src)
                last.then_inc(keys_in, 1)

            pool.wait_ge(chunk_done, C_BR)
            pool.wait_ge(turned_out, 13)
            pool.wait_ge(gate_stored[0], 16 * 8)
            pool.wait_ge(gate_stored[1], 16 * 8)
            load_k(0)
            add_new_keys(0)
            load_v(0)
            with pool.Fori(0, 3) as i:
                for e in range(2):
                    pool.wait_ge(scores, i * NU + (6 + 6 * e))
                    pool.wait_ge(chunk_done, C_BR)
                    load_k(i * 2 + (1 + e))
                    add_new_keys(i * 2 + (1 + e))
                    pool.wait_ge(pv, i * NU + (6 + 6 * e))
                    pool.wait_ge(chunk_done, C_BR)
                    load_v(i * 2 + (1 + e))
            pool.wait_ge(scores, 3 * NU + 6)
            load_k(7)
            add_new_keys(7)
            pool.wait_ge(pv, 3 * NU + 6)
            load_v(7)

            def load_gates(q, e):
                for k in range(2):
                    pool.dma_start(gt[:, 2 * e + k], gates_d[bass.ds(q * 2 + 16 * k, 2)].rearrange("t p n -> p t n")
                                   ).then_inc(g_in[2 * e + k], 16)

            pool.wait_ge(o_out, 4 * NU)
            pool.wait_ge(pv, 4 * NU)
            load_gates(0, 0)
            load_gates(1, 1)
            with pool.Fori(0, 3) as i:
                for e in range(2):
                    pool.wait_ge(m_sum, i * 2 + (1 + e))
                    pool.wait_ge(pv, 4 * NU)
                    load_gates(i * 2 + (2 + e), e)

            def load_x(q, e):
                pool.dma_start(xres[:, e], a["xT"][bass.ds(q * 256, 256)].rearrange("(t p) n -> p t n", p=P)
                               ).then_inc(xr_in[e], 16)

            load_x(0, 0)
            load_x(1, 1)
            with pool.Fori(0, 3) as i:
                pool.wait_ge(evac[1], i + ((G_WO + 1) // 2))
                pool.wait_ge(pv, 4 * NU)
                load_x(i * 2 + 2, 0)
                pool.wait_ge(evac[0], i + ((G_WO + 1) // 2 + 1))
                pool.wait_ge(pv, 4 * NU)
                load_x(i * 2 + 3, 1)

            with pool.Fori(0, DB) as n:
                piece = 0
                for name, win, parts in (("a", 128, 1), ("b1", 128, 1), ("b2", 512, 2), ("b3", 2048, 4)):
                    keep, past = min(win, PAST + DT), min(win, PAST)
                    cache = a[f"cache_{name}_kv"][0]
                    rows = (keep - DT) // parts
                    for q in range(parts):
                        pool.wait_ge(lo_done, n * 30 + (C_FF + 4 * piece))
                        pool.wait_ge(pv, 4 * NU)
                        dst = o[name + "_s"][0, bass.ds(n, 1), q * rows:(q + 1) * rows].rearrange("n t s h d -> (n t) (s h d)")
                        first = past - (keep - DT) + q * rows
                        src = cache[bass.ds(n, 1), first:first + rows].rearrange("n t s h d -> (n t) (s h d)")
                        pool.dma_start(dst, src).then_inc(out_cache, 16)
                        piece += 1
            pool.wait_ge(out_kv, 16 * 12)
            pool.wait_ge(out_cache, 16 * 8 * DB)
            pool.wait_ge(y_out, 16 * 4)

        @block.scalar
        def _(act):
            def split(q, slot, first=False):
                act.wait_ge(loaded[slot], q * 16 + 16)
                if not first:
                    act.wait_ge(chunk_done, q * 4 + (slot - RING + 1))
                act.activation(whi[:, slot], raw[:, slot], ACT.Copy).then_inc(hi_done, 1)

            for j in range(4):
                split(0, j, first=True)
                act.wait_ge(x_in[j], 16)
                act.activation(xhi[:, 4 * j:4 * j + 4], xraw[:, 4 * j:4 * j + 4], ACT.Copy).then_inc(x_hi, 1)

            def turn_out(g, i, c, kind):
                par = c % 2
                act.wait_ge(turned, g - 9)
                ps = psTf[:, 0:768].rearrange("p (c n) -> p c n", c=3)

                def move(dst, dcol, scol, n):
                    act.activation(dst[:, 0:2, dcol], ps[:, 0:2, scol:scol + n], ACT.Copy)
                    return act.activation(dst[0:64, 2, dcol], ps[0:64, 2, scol:scol + n], ACT.Copy)

                def store(src, scol, dcol, n, done=kv_stored[par]):
                    act.dma_start(kvn_d[0:256, bass.ds(dcol, n)].rearrange("(c p) n -> p c n", p=P),
                                  src[:, 0:2, scol]).then_inc(done, 16)
                    act.dma_start(kvn_d[256:NTOK, bass.ds(dcol, n)], src[0:64, 2, scol]).then_inc(done, 16)

                if kind == "kva":
                    move(kst[:, par], slice(0, P), 0, P)
                    move(vnat, slice(0, P), P, P).then_inc(turned_out, 1)
                    act.wait_ge(turned_out, 1)
                    store(kst[:, par], slice(0, P), 0, P)
                    store(vnat, slice(0, P), KVW, P, kv_stored[1])
                elif kind == "k":
                    act.wait_ge(kv_stored[par], i * 32 + {11: 32, 12: 32, 15: 96, 16: 96}[c])
                    move(kst[:, par], slice(0, GW), 0, GW).then_inc(turned_out, 1)
                    act.wait_ge(turned_out, g - 9)
                    store(kst[:, par], slice(0, GW), (g - G_K) * GW + P, GW)
                else:
                    col = bass.ds((g - G_V) * GW + P, GW)
                    move(vnat, col, 0, GW).then_inc(turned_out, 1)
                    act.wait_ge(turned_out, g - 9)
                    store(vnat, col, (g - G_V) * GW + (KVW + P), GW)

            def step(g, i, c, kind, turn):
                par, h = c % 2, i + c // 2
                for j in range(4):
                    split(g + 1, j)
                act.wait_ge(chunk_done, g * 4 + 4)
                ps = psM[par]
                if kind in ("q", "k", "kva"):
                    n = 1 if kind == "kva" else 2
                    if c > 0:
                        act.wait_ge(evac[1 - par], i + ((c - 1) // 2 + 1))
                    for q in range(4):
                        last = act.activation(rot[32 * q:32 * q + 32, 0:n], ps[32 * (q ^ 1):32 * (q ^ 1) + 32, 0:n, 0:NTOK],
                                              ACT.Copy)
                    if kind == "kva":
                        last = act.activation(tT[:, par, 1], ps[:, 1, 0:NTOK], ACT.Copy)
                    last.then_inc(rot_ready, 1)
                elif kind == "v":
                    act.wait_ge(turned, g - 11)
                    if c <= 18:
                        act.wait_ge(kcopy, 7 if c == 18 else 6)
                    act.activation(tT[:, par], ps[:, :, 0:NTOK], ACT.Copy).then_inc(evac[par], 1)
                else:
                    if c > 24:
                        act.wait_ge(gate_stored[par], i * 16 + 16)
                    act.activation(gstage[:, par], ps[:, :, 0:NTOK], ACT.Sigmoid).then_inc(evac[par], 1)
                    act.wait_ge(evac[par], h + 1)
                    act.dma_start(gates_d[bass.ds((g - G_G) * 2, 2)].rearrange("t p n -> p t n"), gstage[:, par]
                                  ).then_inc(gate_stored[par], 16)
                if turn:
                    turn_out(g - 1, i, c - 1, turn)

            projections(act, step)

            def exps(j, k, U):
                kind, e, qb = UNITS[k]
                par = k % 3
                s = st[:, par]
                act.wait_ge(shifted, U + 1)
                nh, n = {"A": (2, P * (qb + 1)), "B": (1, 384 * (qb + 1)), "SB": (1, 3 * KN), "SA": (1, KN)}[kind]
                for hh in range(nh):
                    last = act.activation(S[:, par, hh * n:hh * n + n], S[:, par, hh * n:hh * n + n], ACT.Exp,
                                          bias=s[:, 2 + hh:3 + hh], accum_out=s[:, 4 + hh:5 + hh])
                if k in SINKED:
                    last = act.activation(s[:, 6:6 + nh], s[:, 12:12 + nh], ACT.Exp)
                last.then_inc(exped, 1)

            def turned_probs(j, k, U):
                kind, e, qb = UNITS[k]
                out = PT[:, k % 2]
                act.wait_ge(pT, U + 1)
                if kind in ("A", "B"):
                    n = (384 if kind == "B" else 256) * (qb + 1)
                    act.activation(out[:, 0:n], psTf[:, 0:n], ACT.Copy).then_inc(pT_out, 1)
                else:
                    n, new = (384, NG * DT) if kind == "SB" else (P, DT)
                    act.activation(out[:, 0:n], psTf[:, 0:n], ACT.Copy)
                    act.activation(out[0:new, 512:640], psTf[0:new, 512:640], ACT.Copy).then_inc(pT_out, 1)

            def sums_evac(j, k, U):
                act.wait_ge(sums, j * 2 + (UNITS[k][1] + 1))
                act.activation(PT[:, k % 2, 0:512], psO[:, k % 2], ACT.Copy).then_inc(sums_out, 1)

            def o_evac(j, k, U):
                kind, e, qb = UNITS[k]
                ps = psO[:, k % 2]
                act.wait_ge(pv, U + 1)
                if kind in ("A", "B"):
                    part = slice(64 * e, 64 * e + 64) if kind == "B" else slice(0, P)
                    tile = j + (8 if kind == "B" else 4 * e)
                    last = act.activation(oT[part, bass.ds(tile, 1), P * qb:P * qb + P],
                                          ps[part, 0:P].rearrange("p (a n) -> p a n", a=1), ACT.Copy)
                elif kind == "SB":
                    for hh in range(2):
                        src = ps[64 * hh:64 * hh + 64, 0:64].rearrange("p (a c h e) -> p a h e c", a=4, c=4, h=2)[:, :, hh]
                        dst = oT[64 * hh:64 * hh + 64, 8:12, bass.ds(j * 16 + (SEQ + 8 * e), 8)].rearrange("p a (e c) -> p a e c", e=2)
                        last = act.activation(dst, src, ACT.Copy)
                else:
                    for kv in range(2):
                        for w in range(2):
                            src = ps[64 * kv:64 * kv + 64, 64 * kv:64 * kv + 64].rearrange("p (t w i) -> p t w i", t=4, w=2)[:, :, w]
                            dst = oT[64 * w:64 * w + 64, 4 * kv:4 * kv + 4, bass.ds(j * 16 + (SEQ + 8 * e), 8)]
                            last = act.activation(dst, src, ACT.Copy)
                last.then_inc(o_out, 1)

            exps(0, 0, 0)

            def attend(at):
                if at(1):
                    exps(*at(1))
                if at(-2) and UNITS[at(-2)[1]][0] == "SB":
                    o_evac(*at(-2))
                if at(-1):
                    (sums_evac if UNITS[at(-1)[1]][0] == "SB" else o_evac)(*at(-1))
                turned_probs(*at(0))

            units(act, attend)
            o_evac(3, NU - 2, 4 * NU - 2)
            o_evac(3, NU - 1, 4 * NU - 1)

            act.wait_ge(o_out, 4 * NU)
            for j in range(3):
                act.activation(ohi[:, 4 * j:4 * j + 4], oT[:, 4 * j:4 * j + 4], ACT.Copy).then_inc(o_hi, 1)

            with act.Fori(0, 2) as i:
                for q in range(4):
                    for j in range(3):
                        s = 3 * q + j
                        split(i * 3 + (C_BR // 4 + 1 + s // 4), s % 4)
                    act.wait_ge(m_sum, i * 4 + (q + 1))
                    act.activation(mhi[:, bass.ds(i * 8 + 2 * q, 2)], t2[:, q % 2], ACT.Copy).then_inc(m_hi, 1)

            with act.Fori(0, 8) as i:
                for j in range(4):
                    split(i + (C_WO // 4 + 1), j)

            def layer_norm(li, gam, bet):
                act.activation(eps[:, 1:2], eps[:, 0:1], ACT.Sqrt)
                for p in range(4):
                    act.wait_ge(centred, 4 * li + p + 1)
                    act.activation(squares[p], r[:, 4 * p:4 * p + 4], ACT.Square).then_inc(squared, 1)
                act.wait_ge(var_ready, li + 1)
                act.activation(lnrow[:, 2], psT[:, 1, 0:NTOK], ACT.Sqrt, bias=eps[:, 0:1]).then_inc(rooted, 1)
                for p in range(4):
                    act.wait_ge(scaled, 4 * li + p + 1)
                    for t in range(4 * p + 2, 4 * p + 4):
                        last = act.activation(r[:, t], r[:, t], ACT.Identity, bias=bet[:, t:t + 1], scale=gam[:, t:t + 1])
                    last.then_inc(affine_a, 1)
                    act.wait_ge(affine_a, 4 * li + p + 1)
                    act.wait_ge(affine_d, 4 * li + p + 1)
                    if li == 0:
                        act.activation(hhi[:, 4 * p:4 * p + 4], r[:, 4 * p:4 * p + 4], ACT.Copy).then_inc(h_hi, 1)
                    else:
                        act.dma_start(o["yT"].rearrange("(t p) n -> p t n", p=P)[:, 4 * p:4 * p + 4],
                                      r[:, 4 * p:4 * p + 4]).then_inc(y_out, 16)

            layer_norm(0, ln1g, ln1b)

            def up(b, q, c):
                par = 1 - c
                for j in range(4):
                    split(b * 16 + q * 2 + (C_FF // 4 + 1 + c), j)
                act.wait_ge(chunk_done, b * C_BLK + q * 8 + (C_FF + 4 * c + 4))
                for t in range(2):
                    last = act.activation(t2[:, c, t], psM[par][:, t, 0:NTOK], ACT.Relu,
                                          bias=bff1[:, bass.ds(b * 16 + q * 4 + (2 * c + t), 1)])
                last.then_inc(evac[par], 1)
                act.wait_ge(u_done, b * 8 + q * 2 + (c + 1))
                act.activation(uhi[:, bass.ds(q * 4 + 2 * c, 2)], t2[:, c], ACT.Copy).then_inc(u_hi, 1)

            with act.Fori(0, 3) as b:
                with act.Fori(0, 4) as q:
                    up(b, q, 0)
                    up(b, q, 1)
                with act.Fori(0, 8) as q:
                    for j in range(4):
                        split(b * 16 + q + (C_FF // 4 + 9), j)
            with act.Fori(0, 4) as q:
                up(3, q, 0)
                up(3, q, 1)
            with act.Fori(0, 7) as q:
                for j in range(4):
                    split(q + (3 * 16 + C_FF // 4 + 9), j)
            layer_norm(1, ln2g, ln2b)

        @block.vector
        def _(dve):
            def split(q, slot, first=False):
                dve.wait_ge(hi_done, q * 4 + (slot + 1))
                if not first:
                    dve.wait_ge(chunk_done, q * 4 + (slot - RING + 1))
                dve.tensor_tensor(wlo[:, slot], raw[:, slot], whi[:, slot].bitcast(F32), ALU.subtract).then_inc(lo_done, 1)

            for j in range(4):
                split(0, j, first=True)
                dve.wait_ge(x_hi, j + 1)
                dve.tensor_tensor(xlo[:, 4 * j:4 * j + 4], xraw[:, 4 * j:4 * j + 4],
                                  xhi[:, 4 * j:4 * j + 4].bitcast(F32), ALU.subtract).then_inc(x_lo, 1)
            dve.wait_ge(const_in, 16 * 8)

            def stage(j, k, U):
                kind, e, qb = UNITS[k]
                if k == 0:
                    wait(dve, pv, U - 4)
                    q4, k4 = (t.rearrange("p (g a) n -> p g a n", g=3) for t in (qTb, kTb[:, :, :]))
                    dve.tensor_copy(QB[:], q4[:, :, bass.ds(j, 1), 0:256].rearrange("p g a n -> p g (a n)"))
                    dve.tensor_copy(KB[:], k4[:, :, bass.ds(j, 1), 0:256].rearrange("p g a n -> p g (a n)"))
                    for kb in range(2):
                        last = dve.tensor_copy(VB[:, kb], vnat[:, kb, P:KVW].rearrange("p (g n) -> p g n", g=3)[:, :, bass.ds(j * P, P)])
                elif k == 2:
                    q2 = qTa.rearrange("p (a b) n -> p a b n", a=2)
                    last = dve.tensor_copy(QA[:], q2[:, :, bass.ds(j, 1), 0:256].rearrange("p a b n -> p a (b n)"))
                elif kind == "SB":
                    for g in range(3):
                        for hh in range(2):
                            src = qTb[64 * hh:64 * hh + 64, 4 * g:4 * g + 4, bass.ds(j * 16 + (SEQ + 8 * e), 8)].rearrange("p a (e c) -> p a c e", e=2)
                            at = 512 * g + 2 * hh
                            dst = QbS[64 * hh:64 * hh + 64, at:at + 4 * 132].rearrange("p (a x) -> p a x", a=4)[:, :, 0:P]
                            last = dve.tensor_copy(dst.rearrange("p a (c w) -> p a c w", c=4)[:, :, :, 0:2], src)
                elif kind == "SA":
                    for kv in range(2):
                        for w in range(2):
                            dst = QaS[64 * kv:64 * kv + 64, 64 * kv:64 * kv + 64].rearrange("p (t w i) -> p t w i", t=4, w=2)[:, :, w]
                            src = qTa[64 * w:64 * w + 64, 4 * kv:4 * kv + 4, bass.ds(j * 16 + (SEQ + 8 * e), 8)]
                            last = dve.tensor_copy(dst, src)
                else:
                    return
                last.then_inc(staged, 1)

            def stage_first():
                dve.wait_ge(turned_out, 13)
                dve.wait_ge(kcopy, 7)
                dve.wait_ge(kv_stored[0], 16 * 14)
                dve.wait_ge(kv_stored[1], 16 * 14)
                dve.memset(QbS[:], 0.0)
                dve.memset(QaS[:], 0.0).then_inc(zeroed, 1)
                dve.wait_ge(zeroed, 2)
                for k in range(4):
                    stage(0, k, k)


            def step(g, i, c, kind, turn):
                par, h = c % 2, i + c // 2
                for j in range(4):
                    split(g + 1, j)
                if c == 24:
                    stage_first()
                if kind in ("v", "gate"):
                    return
                n = 1 if kind == "kva" else 2
                dst = {"q": lambda: qT[:, bass.ds(g * 2, 2)],
                       "k": lambda: tT[:, par], "kva": lambda: tT[:, par, 0:1]}[kind]()
                cos, sin = (rope[:, k:k + 1].broadcast_to([P, n, NTOK]) for k in range(2))
                dve.wait_ge(chunk_done, g * 4 + 4)
                if kind == "k" and c > 11:
                    dve.wait_ge(turned, g - 11)
                    dve.wait_ge(kcopy, g - 11)
                dve.wait_ge(rot_ready, g + 1)
                dve.tensor_tensor(dst, psM[par][:, 0:n, 0:NTOK], cos, ALU.mult).then_inc(rope_a, 1)
                dve.tensor_tensor(rot[:, 0:n], rot[:, 0:n], sin, ALU.mult).then_inc(rope_b, 1)
                dve.wait_ge(rope_a, g + 1)
                dve.wait_ge(rope_b, g + 1)
                dve.tensor_tensor(dst, dst, rot[:, 0:n], ALU.add).then_inc(evac[par], 1)
                if kind == "kva":
                    dve.wait_ge(evac[par], h + 1)
                    src = tT[:, par, 0]
                    dve.tensor_copy(kTa[:, 0], src)
                    for kv in range(2):
                        for half in range(2):
                            last = dve.tensor_copy(kTa[64 * half:64 * half + 64, 1 + kv], src[64 * kv:64 * kv + 64])
                    last.then_inc(kcopy, 1)

            projections(dve, step)

            def front(j, k, U):
                kind, e, qb = UNITS[k]
                par = k % 2
                ps = psM[par][:, :, :].rearrange("p a (b n) -> p (a b) n", b=2)
                s, Sp = st[:, k % 3], S[:, k % 3]
                nk = P * (qb + 1)
                pm = mask_p[:, :, 256 - nk:256]
                dve.wait_ge(scores, U + 1)
                wait(dve, pT, U - 2)
                if kind == "B":
                    nh, n = 1, 3 * nk
                    last = dve.scalar_tensor_tensor(Sp[:, 0:n].rearrange("p (g k) -> p g k", g=3), ps[:, 0:3, 0:nk], SCALE, pm,
                                                    ALU.mult, ALU.add)
                elif kind == "A":
                    nh, n = 2, nk
                    for hh in range(2):
                        last = dve.scalar_tensor_tensor(Sp[:, hh * nk:hh * nk + nk], ps[:, 2 * hh, 0:nk], SCALE, pm[:, 0], ALU.mult, ALU.add)
                else:
                    b0, nb = (0, 3) if kind == "SB" else (3, 1)
                    nh, n = 1, KN * nb
                    cached, new = Sp[:, 0:P * nb], Sp[:, P * nb:KN * nb]
                    dve.scalar_tensor_tensor(cached.rearrange("p (g k) -> p g k", g=nb), ps[:, 0:nb, 0:P], SCALE,
                                             mask_c[:, b0:b0 + nb], ALU.mult, ALU.add)
                    last = dve.scalar_tensor_tensor(new.rearrange("p (g k) -> p g k", g=nb), ps[:, 0:nb, P:KN], SCALE,
                                                    mask_n[:, b0:b0 + nb], ALU.mult, ALU.add)
                last.then_inc(masked, 1)
                dve.wait_ge(masked, U + 1)
                dve.tensor_reduce(s[:, 0:nh], Sp[:, 0:nh * n].rearrange("p (h k) -> p h k", h=nh), AX.X, ALU.max).then_inc(maxed, 1)
                dve.wait_ge(maxed, U + 1)
                if k not in SINKED:
                    dve.tensor_scalar(s[:, 2:3], s[:, 0:1], -1.0, None, ALU.mult).then_inc(shifted, 1)
                    return
                sink = sink_p[:, bass.ds(j * 2 + 8 * e, 2)] if kind == "A" else sink_s[:]
                dve.tensor_tensor(s[:, 0:nh], s[:, 0:nh], sink, ALU.max).then_inc(sinkmax, 1)
                dve.wait_ge(sinkmax, j * NSINK + SINKED[k])
                dve.tensor_scalar(s[:, 2:2 + nh], s[:, 0:nh], -1.0, None, ALU.mult)
                dve.tensor_tensor(s[:, 12:12 + nh], sink, s[:, 0:nh], ALU.subtract).then_inc(shifted, 1)

            def back(j, k, U):
                kind, e, qb = UNITS[k]
                s, Sp = st[:, k % 3], S[:, k % 3]
                nh, n = {"A": (2, P * (qb + 1)), "B": (1, 384 * (qb + 1)), "SB": (1, 3 * KN), "SA": (1, KN)}[kind]
                dve.wait_ge(exped, U + 1)
                total = s[:, 4:4 + nh]
                if k in SINKED:
                    total = s[:, 8:8 + nh]
                    dve.tensor_tensor(total, s[:, 4:4 + nh], s[:, 6:6 + nh], ALU.add).then_inc(denom, 1)
                    dve.wait_ge(denom, j * NSINK + SINKED[k])
                dve.reciprocal(s[:, 10:10 + nh], total).then_inc(recip, 1)
                dve.wait_ge(recip, U + 1)
                for hh in range(nh):
                    last = dve.tensor_scalar(Sp[:, hh * n:hh * n + n], Sp[:, hh * n:hh * n + n], s[:, 10 + hh:11 + hh], None, ALU.mult)
                last.then_inc(normed, 1)

            front(0, 0, 0)
            dve.wait_ge(gate_stored[0], 16 * 8)
            dve.wait_ge(gate_stored[1], 16 * 8)

            def attend(at):
                if at(1):
                    front(*at(1))
                back(*at(0))
                if at(4) and at(4)[1] != 0:
                    stage(*at(4))
                if at(3) and at(3)[1] == 0:
                    stage(*at(3))

            units(dve, attend)

            for j in range(3):
                dve.wait_ge(o_hi, j + 1)
                dve.tensor_tensor(olo[:, 4 * j:4 * j + 4], oT[:, 4 * j:4 * j + 4], ohi[:, 4 * j:4 * j + 4].bitcast(F32),
                                  ALU.subtract).then_inc(o_lo, 1)

            with dve.Fori(0, 2) as i:
                for q in range(4):
                    c0 = C_BR + 3 * q
                    for j in range(2):
                        s = 3 * q + j
                        split(i * 3 + (C_BR // 4 + 1 + s // 4), s % 4)
                    dve.wait_ge(chunk_done, i * 12 + (c0 + 2))
                    dve.wait_ge(g_in[2 * (q % 2)], i * 32 + 16 * (q // 2 + 1))
                    dve.tensor_tensor(t1[:], psM[1][:, :, 0:NTOK], gt[:, 2 * (q % 2)], ALU.mult).then_inc(evac[1], 1)
                    s = 3 * q + 2
                    split(i * 3 + (C_BR // 4 + 1 + s // 4), s % 4)
                    dve.wait_ge(chunk_done, i * 12 + (c0 + 3))
                    dve.wait_ge(g_in[2 * (q % 2) + 1], i * 32 + 16 * (q // 2 + 1))
                    dve.tensor_tensor(t2[:, q % 2], psM[0][:, :, 0:NTOK], gt[:, 2 * (q % 2) + 1], ALU.mult).then_inc(evac[0], 1)
                    dve.wait_ge(evac[1], i * 4 + (q + G_BR // 2 + 1))
                    dve.wait_ge(evac[0], i * 4 + (q + (G_BR + 1) // 2 + 1))
                    dve.tensor_tensor(t2[:, q % 2], t1[:], t2[:, q % 2], ALU.add).then_inc(m_sum, 1)
                    dve.wait_ge(m_hi, i * 4 + (q + 1))
                    dve.tensor_tensor(mlo[:, bass.ds(i * 8 + 2 * q, 2)], t2[:, q % 2], mhi[:, bass.ds(i * 8 + 2 * q, 2)].bitcast(F32),
                                      ALU.subtract).then_inc(m_lo, 1)

            def add_sum(pair, group, n):
                dve.wait_ge(*group)
                dve.wait_ge(summed, n - 1)
                dve.tensor_tensor(lnrow[:, 0:2], lnrow[:, 0:2], pair, ALU.add).then_inc(summed, 1)

            dve.memset(lnrow[:, 0:2], 0.0).then_inc(summed, 1)
            with dve.Fori(0, 4) as i:
                for c in range(2):
                    for j in range(4):
                        split(i * 2 + (C_WO // 4 + 1 + c), j)
                    dve.wait_ge(chunk_done, i * 8 + (C_WO + 4 * c + 4))
                    dve.wait_ge(xr_in[c], i * 16 + 16)
                    pair = r[:, bass.ds(i * 4 + 2 * c, 2)]
                    dve.scalar_tensor_tensor(pair, xres[:, c], ALPHA, psM[1 - c][:, :, 0:NTOK],
                                             ALU.mult, ALU.add).then_inc(evac[1 - c], 1)
                    add_sum(pair, (evac[1 - c], i + ((G_WO + c) // 2 + 1)), i * 2 + (c + 2))

            def layer_norm(li, gam, bet):
                part = [r[:, 4 * p:4 * p + 4] for p in range(4)]

                def pair_up(p):
                    dve.wait_ge(squared, 4 * li + p + 1)
                    dve.tensor_tensor(squares[p][:, 0:2], squares[p][:, 0:2], squares[p][:, 2:4], ALU.add).then_inc(paired, 1)
                    dve.wait_ge(paired, 4 * li + p + 1)
                    dve.tensor_tensor(squares[p][:, 0], squares[p][:, 0], squares[p][:, 1], ALU.add).then_inc(added, 1)

                def low(p):
                    dve.wait_ge(h_hi, p + 1)
                    dve.tensor_tensor(hlo[:, 4 * p:4 * p + 4], part[p], hhi[:, 4 * p:4 * p + 4].bitcast(F32),
                                      ALU.subtract).then_inc(h_lo, 1)

                dve.wait_ge(mean_ready, li + 1)
                for p in range(4):
                    dve.tensor_tensor(part[p], part[p], psT[:, 0:1, 0:NTOK].broadcast_to([P, 4, NTOK]), ALU.subtract).then_inc(centred, 1)
                    if p >= 2:
                        pair_up(p - 2)
                pair_up(2)
                pair_up(3)
                dve.wait_ge(rooted, li + 1)
                dve.reciprocal(lnrow[:, 0], lnrow[:, 2]).then_inc(rstd, 1)
                dve.wait_ge(rstd, li + 1)
                for p in range(4):
                    dve.tensor_tensor(part[p], part[p], lnrow[:, 0:1].broadcast_to([P, 4, NTOK]), ALU.mult).then_inc(scaled, 1)
                    if li == 0 and p >= 1:
                        low(p - 1)
                    dve.wait_ge(scaled, 4 * li + p + 1)
                    for t in range(4 * p, 4 * p + 2):
                        last = dve.tensor_scalar(r[:, t], r[:, t], gam[:, t:t + 1], bet[:, t:t + 1], ALU.mult, ALU.add)
                    last.then_inc(affine_d, 1)
                if li == 0:
                    low(3)

            layer_norm(0, ln1g, ln1b)
            dve.wait_ge(h_lo, 4)
            for t in range(16):
                last = dve.tensor_scalar(r[:, t], r[:, t], ALPHA, bff2[:, t:t + 1], ALU.mult, ALU.add)
            last.then_inc(r_init, 1)
            dve.wait_ge(r_init, 1)

            def up(b, q, c):
                for j in range(4):
                    split(b * 16 + q * 2 + (C_FF // 4 + 1 + c), j)
                dve.wait_ge(evac[1 - c], b * 8 + q + ((G_FF + c) // 2 + 1))
                dve.tensor_tensor(t2[:, c], t2[:, c], t2[:, c], ALU.mult).then_inc(u_done, 1)
                dve.wait_ge(u_hi, b * 8 + q * 2 + (c + 1))
                part = bass.ds(q * 4 + 2 * c, 2)
                dve.tensor_tensor(ulo[:, part], t2[:, c], uhi[:, part].bitcast(F32), ALU.subtract).then_inc(u_lo, 1)

            def down(b, q, c, last=False):
                if not last:
                    for j in range(4):
                        split(b * 16 + q * 2 + (C_FF // 4 + 9 + c), j)
                dve.wait_ge(chunk_done, b * C_BLK + q * 8 + (C_FF + 32 + 4 * c + 4))
                part = r[:, bass.ds(q * 4 + 2 * c, 2)]
                dve.tensor_tensor(part, part, psM[1 - c][:, :, 0:NTOK], ALU.add).then_inc(evac[1 - c], 1)
                if isinstance(b, int):
                    add_sum(part, (evac[1 - c], b * 8 + q + ((G_FF + 8 + c) // 2 + 1)), q * 2 + (9 + c + 2))

            with dve.Fori(0, 3) as b:
                with dve.Fori(0, 4) as q:
                    up(b, q, 0)
                    up(b, q, 1)
                with dve.Fori(0, 4) as q:
                    down(b, q, 0)
                    down(b, q, 1)
            dve.memset(lnrow[:, 0:2], 0.0).then_inc(summed, 1)
            with dve.Fori(0, 4) as q:
                up(3, q, 0)
                up(3, q, 1)
            with dve.Fori(0, 3) as q:
                down(3, q, 0)
                down(3, q, 1)
            down(3, 3, 0)
            down(3, 3, 1, last=True)
            layer_norm(1, ln2g, ln2b)

        @block.tensor
        def _(pe):
            def chunk(c, slot, ps, hi, lo, t0, first, last):
                pe.wait_ge(lo_done, c + 1)
                for k in range(KT):
                    for t in range(2):
                        wh, wl = (w[:, slot, k, P * t:P * t + P] for w in (whi, wlo))
                        out = ps[:, t, 0:NTOK]
                        pe.matmul(out, wh, hi[:, t0 + k], start=first and k == 0, stop=False)
                        pe.matmul(out, wh, lo[:, t0 + k], start=False, stop=False)
                        mm = pe.matmul(out, wl, hi[:, t0 + k], start=False, stop=last and k == KT - 1)
                mm.then_inc(chunk_done, 1)

            def group(c, ps, hi, lo, ready=None):
                for j in range(4):
                    if ready is not None:
                        pe.wait_ge(*ready(j))
                    chunk(c + j, j, ps, hi, lo, 4 * j, j == 0, j == 3)

            def turn(g, i, c):
                par = c % 2
                pe.wait_ge(evac[par], i + (c // 2 + 1))
                if c > 10:
                    pe.wait_ge(turned_out, g - 10)
                for k in range(3):
                    n = P if k < 2 else 64
                    for t in range(2):
                        mm = pe.transpose(psTf[0:n, k * GW + t * P:k * GW + t * P + P], tT[:, par, t, k * P:k * P + n], ident[:])
                mm.then_inc(turned, 1)

            def step(g, i, c, kind, turned_kind):
                par, h = c % 2, i + c // 2
                if c >= 2:
                    pe.wait_ge(evac[par], h)
                if c == 0:
                    group(g * 4, psM[par], xhi, xlo, ready=lambda j: (x_lo, j + 1))
                else:
                    group(g * 4, psM[par], xhi, xlo)
                if turned_kind:
                    if c == 11:
                        pe.wait_ge(const_in, 16 * 8)
                    turn(g - 1, i, c - 1)

            projections(pe, step)

            def unit_scores(j, k, U):
                kind, e, qb = UNITS[k]
                ps = psM[k % 2][:, :, :].rearrange("p a (b n) -> p (a b) n", b=2)
                if k in STAGED:
                    pe.wait_ge(staged, j * NSTAGE + STAGED[k])
                wait(pe, masked, U - 1)
                nk, qs = P * (qb + 1), slice(P * qb, P * qb + P)
                if kind == "B":
                    for g in range(3):
                        mm = pe.matmul(ps[:, g, 0:nk], QB[64 * e:64 * e + 64, g, qs], KB[64 * e:64 * e + 64, g, 0:nk],
                                       start=True, stop=True)
                elif kind == "A":
                    for hh in range(2):
                        mm = pe.matmul(ps[:, 2 * hh, 0:nk], QA[64 * hh:64 * hh + 64, e, qs], kTa[64 * hh:64 * hh + 64, 1 + e, 0:nk],
                                       start=True, stop=True)
                elif kind == "SB":
                    pe.wait_ge(keys_in, j * 2 + (e + 1))
                    for pr in range(4):
                        mm = pe.matmul(ps[:, 0, 0:KN], Qb[:, 0, pr], kcache[:, pr, 0], start=pr == 0, stop=pr == 3)
                    for g in range(1, 3):
                        for pr in range(4):
                            for c in range(4):
                                mm = pe.matmul(ps[32 * c:32 * c + 32, g, 0:KN], Qb[:, g, pr, 32 * c:32 * c + 32],
                                               kcache[:, pr, 4 * g - 3 + c], start=pr == 0, stop=pr == 3)
                else:
                    mm = pe.matmul(ps[:, 0, 0:KN], QaS[:], kca[:], start=True, stop=True)
                mm.then_inc(scores, 1)

            def turn_probs(j, k, U):
                kind, e, qb = UNITS[k]
                Sp = S[:, k % 3]
                pe.wait_ge(normed, U + 1)
                wait(pe, pT_out, U)
                if kind in ("A", "B"):
                    for t in range((3 if kind == "B" else 2) * (qb + 1)):
                        mm = pe.transpose(psTf[:, t * P:t * P + P], Sp[:, t * P:t * P + P], ident[:])
                else:
                    full, new = (3, NG * DT) if kind == "SB" else (1, DT)
                    for t in range(full):
                        pe.transpose(psTf[:, t * P:t * P + P], Sp[:, t * P:t * P + P], ident[:])
                    mm = pe.transpose(psTf[0:new, 512:640], Sp[:, full * P:full * P + new], ident[:])
                mm.then_inc(pT, 1)

            def unit_values(j, k, U):
                kind, e, qb = UNITS[k]
                out, PTk, nb = psO[:, k % 2], PT[:, k % 2], 3 * (qb + 1)
                if kind in ("SB", "SA"):
                    pe.wait_ge(vc_in, j * 192 + 96 * (e + 1))
                pe.wait_ge(pT_out, U + 1)
                wait(pe, o_out, U - 1)
                if kind == "B":
                    for t in range(nb):
                        g, kb = divmod(t, qb + 1)
                        mm = pe.matmul(out[64 * e:64 * e + 64, 0:P], VB[:, kb, g, 64 * e:64 * e + 64], PTk[:, t * P:t * P + P],
                                       start=t == 0, stop=t == nb - 1)
                elif kind == "A":
                    for hh in range(2):
                        for kb in range(qb + 1):
                            t = hh * (qb + 1) + kb
                            mm = pe.matmul(out[64 * hh:64 * hh + 64, 0:P], vnat[:, kb, 64 * e:64 * e + 64], PTk[:, t * P:t * P + P],
                                           start=kb == 0, stop=kb == qb)
                elif kind == "SB":
                    pe.matmul(out, PTk[:, 0:P], vcache[:, 0], start=True, stop=False, skip_group_check=True)
                    for g in range(1, 3):
                        for c in range(4):
                            pe.matmul(out[32 * c:32 * c + 32], PTk[:, P * g + 32 * c:P * g + 32 * c + 32], vcache[:, 4 * g - 3 + c],
                                      start=False, stop=False, skip_group_check=True)
                    pe.matmul(out, PTk[0:NG * DT, 512:640], vnewb[:], start=False, stop=True,
                              skip_group_check=True).then_inc(sums, 1)
                    return
                else:
                    pe.matmul(out[:, 0:P], vca[:], PTk[:, 0:P], start=True, stop=False)
                    mm = pe.matmul(out[:, 0:P], vnewa[:], PTk[0:DT, 512:640], start=False, stop=True)
                mm.then_inc(pv, 1)

            def turn_sums(j, k, U):
                pe.wait_ge(sums_out, j * 2 + (UNITS[k][1] + 1))
                rows = ident[:, :].rearrange("p (c w) -> p c w", c=4)
                for pr in range(4):
                    mm = pe.matmul(psO[:, k % 2, 16 * pr:16 * pr + 16].rearrange("p (c w) -> p c w", c=4),
                                   PT[:, k % 2, P * pr:P * pr + P], rows[:, :, 4 * pr:4 * pr + 4], start=True, stop=True)
                mm.then_inc(pv, 1)

            pe.wait_ge(evac[0], G_BR // 2 + 1)
            pe.wait_ge(evac[1], G_BR // 2)
            unit_scores(0, 0, 0)
            unit_scores(0, 1, 1)

            def attend(at):
                if at(2):
                    unit_scores(*at(2))
                if at(-2) and UNITS[at(-2)[1]][0] == "SB":
                    turn_sums(*at(-2))
                if at(-1):
                    unit_values(*at(-1))
                turn_probs(*at(0))

            units(pe, attend)
            turn_sums(3, NU - 2, 4 * NU - 2)
            unit_values(3, NU - 1, 4 * NU - 1)

            with pe.Fori(0, 2) as i:
                for q in range(4):
                    s = 3 * q
                    pe.wait_ge(evac[1], i * 4 + (q + G_BR // 2))
                    for j in range(2):
                        pe.wait_ge(o_lo, j + 1)
                        chunk(i * 12 + (C_BR + s + j), (s + j) % 4, psM[1], ohi, olo, 4 * j, j == 0, j == 1)
                    pe.wait_ge(evac[0], i * 4 + (q + G_BR // 2 + 1))
                    pe.wait_ge(o_lo, 3)
                    chunk(i * 12 + (C_BR + s + 2), (s + 2) % 4, psM[0], ohi, olo, 8, True, True)

            with pe.Fori(0, 4) as i:
                for c in range(2):
                    pe.wait_ge(evac[1 - c], i + ((G_WO + c) // 2))
                    group(i * 8 + (C_WO + 4 * c), psM[1 - c], mhi, mlo, ready=lambda j: (m_lo, 2 * j + 2))

            def layer_norm(li):
                pe.wait_ge(summed, 9 * li + 9)
                for t in range(2):
                    mm = pe.matmul(psT[:, 0, 0:NTOK], onesD[:], lnrow[:, t], start=t == 0, stop=t == 1)
                mm.then_inc(mean_ready, 1)
                for p in range(4):
                    pe.wait_ge(added, 4 * li + p + 1)
                    mm = pe.matmul(psT[:, 1, 0:NTOK], onesD[:], squares[p][:, 0], start=p == 0, stop=p == 3)
                mm.then_inc(var_ready, 1)

            layer_norm(0)

            with pe.Fori(0, 4) as b:
                with pe.Fori(0, 4) as q:
                    for c in range(2):
                        pe.wait_ge(evac[1 - c], b * 8 + q + ((G_FF + c) // 2))
                        group(b * C_BLK + q * 8 + (C_FF + 4 * c), psM[1 - c], hhi, hlo, ready=lambda j: (h_lo, j + 1))
                with pe.Fori(0, 4) as q:
                    for c in range(2):
                        pe.wait_ge(evac[1 - c], b * 8 + q + ((G_FF + 8 + c) // 2))
                        group(b * C_BLK + q * 8 + (C_FF + 32 + 4 * c), psM[1 - c], uhi, ulo,
                              ready=lambda j: (u_lo, b * 8 + (2 * j + 2)))
            layer_norm(1)


_CACHES = ["cache_a_kv", "cache_b1_kv", "cache_b2_kv", "cache_b3_kv"]
_WEIGHTS = ["w_in", "w_branch_a", "w_branch_b", "w_out", "w_ff1", "w_ff2"]
_OUTS = {
    "yT": (D, NTOK),
    "a_p": (1, 1, 128, 2, 2, HD), "a_s": (1, DB, 128, 2, 2, HD),
    "b1_p": (1, 1, 128, 2, 8, HD), "b1_s": (1, DB, 128, 2, 8, HD),
    "b2_p": (1, 1, 256, 2, 8, HD), "b2_s": (1, DB, 512, 2, 8, HD),
    "b3_p": (1, 1, 256, 2, 8, HD), "b3_s": (1, DB, 1032, 2, 8, HD),
}


def constants():
    half = HD // 2
    inv = (1.0 / (np.float32(THETA) ** (np.arange(half, dtype=np.float32) / np.float32(half)))).astype(np.float32)
    pos = np.concatenate([np.arange(SEQ), np.tile(PAST + np.arange(DT), DB)]).astype(np.float32)
    ang = (pos[None, :] * inv[:, None]).astype(np.float32)
    cos, sin = np.cos(ang.astype(np.float64)), np.sin(ang.astype(np.float64))
    rope = np.stack([np.tile(cos, (4, 1)), np.tile(np.concatenate([-sin, sin]), (2, 1))], 1).astype(np.float32)

    mask_p = np.full((P, NG, 256), NEG, np.float32)
    q, s = np.arange(P)[:, None], np.arange(256)[None, :]
    for g, dil in enumerate(DIL):
        dist = P + q - s
        mask_p[:, g] = np.where((dist >= 0) & (dist % dil == 0) & (dist < 128 * dil), 0, NEG)

    mask_c = np.full((P, 4, P), NEG, np.float32)
    mask_n = np.full((P, 4, DT), NEG, np.float32)
    key = np.arange(P)
    for row in range(P):
        c, w = divmod(row, 32)
        if w < 16:
            i = c + 4 * (w % 2)
            mask_c[row, 0] = np.where(P + i - key < 128, 0, NEG)
            mask_c[row, 1] = np.where(512 + i - (4 * key + c) < 512, 0, NEG)
            mask_c[row, 2] = np.where(4 * (key % 2) + c == i, 0, NEG)
            for g, dil in enumerate(DIL):
                for t in range(DT):
                    if t <= i and (i - t) % dil == 0:
                        mask_n[row, g, t] = 0
        i = row % 8
        mask_c[row, 3] = np.where(P + i - key < 128, 0, NEG)
        mask_n[row, 3, 0:i + 1] = 0
    return {"rope": rope, "ident": np.eye(P, dtype=np.float32), "mask_p": mask_p, "mask_c": mask_c, "mask_n": mask_n}


def layouts(inputs):
    c = np.ascontiguousarray
    tiles = lambda v: v.reshape(-1, P).T
    x = np.concatenate([inputs["x_prompt"].reshape(SEQ, D), inputs["x_sample"].reshape(DB * DT, D)])
    ka, k1, k2, k3 = (inputs[n][0, :, :, 0] for n in _CACHES)
    va, v1, v2, v3 = (inputs[n][0, :, :, 1] for n in _CACHES)

    def chunks(t1, t2, t3):
        t3 = t3.reshape(DB, 64, 4, 4, H_B, HD)[:, :, 0:2].reshape(DB, P, 4, H_B, HD)
        return np.concatenate([t1[:, :, None], t2.reshape(DB, P, 4, H_B, HD), t3], 2)

    kT_b = np.pad(chunks(k1, k2, k3).reshape(DB, P, CK, 4, P).transpose(0, 4, 3, 2, 1), [(0, 0)] * 4 + [(0, DT)])
    sinks = inputs["a_sinks"].reshape(QH_A)
    sink_s = np.repeat(sinks, DT)[:, None]
    out = {
        "xT": c(x.T), "kT_b": c(kT_b).reshape(DB, P, 4 * CK * KN), "v_b": chunks(v1, v2, v3).reshape(DB, P, CK * 512),
        "kT_a": c(np.pad(ka.reshape(DB, P, P).transpose(0, 2, 1), [(0, 0), (0, 0), (0, DT)])),
        "sink_p": c(np.broadcast_to(sinks, (P, QH_A))), "sink_s": c(sink_s),
        "vecs": c(np.concatenate([tiles(inputs[n][0]) for n in ("ln1_g", "ln1_b", "ln2_g", "ln2_b", "b_ff2", "b_ff1")], 1)),
    }
    out.update({n: c(inputs[n]) for n in _CACHES + _WEIGHTS})
    return out


def kernel(**inputs):
    import concourse.bacc as _bacc
    from concourse.bass_utils import run_bass_kernel_spmd as _run

    inputs = {n: np.asarray(v) for n, v in inputs.items()}
    nc = _bacc.Bacc("TRN2", target_bir_lowering=False, num_devices=1)
    arrays, ins, outs = {}, {}, {}
    for name, v in {**layouts(inputs), **constants()}.items():
        arrays[f"in_{name}_dram"] = v
        ins[name] = nc.dram_tensor(f"in_{name}_dram", v.shape, mybir.dt.from_np(v.dtype), kind="ExternalInput").ap()
    for name, shape in _OUTS.items():
        outs[name] = nc.dram_tensor(f"out_{name}_dram", shape, F32, kind="ExternalOutput").ap()
    program(nc, ins, outs)
    got = _run(nc, [arrays], core_ids=[0]).results[0]
    g = {name: got[f"out_{name}_dram"] for name in _OUTS}
    y = np.ascontiguousarray(g["yT"].T)
    return (y[:SEQ].reshape(1, SEQ, D), y[SEQ:].reshape(DB, DT, D), g["a_p"], g["a_s"], g["b1_p"], g["b1_s"],
            g["b2_p"], g["b2_s"], g["b3_p"], g["b3_s"])
```
